# Optimizing a Trainium2 kernel written in Bass

```python
import math
import numpy as np
import jax
import jax.numpy as jnp
from jax import lax

D_MODEL = 1024
BATCH = 1
SEQ = 512
DEPTH = 1

HEAD_DIM = 64
NSA_HEADS = 8
NSA_KV_HEADS = 2
NSA_REP = NSA_HEADS // NSA_KV_HEADS
CMP_LEN = 32
CMP_STRIDE = 16
CMP_HIDDEN = 256
SLC_LEN = 64
SLC_COUNT = 16
WINDOW = 512
DSA_HEADS = 8
KV_LATENT = 128
IDX_HEADS = 8
IDX_DIM = 64
IDX_TOPK_MAX = 256
N_HEADS_TOTAL = NSA_HEADS + DSA_HEADS
MIX_WIDTH = N_HEADS_TOTAL * HEAD_DIM
N_BUCKETS = 32
BUCKET_EXACT = 16
BUCKET_MAX_DIST = 128
N_EXPERTS = 32
TOP_K = 4
D_EXPERT = D_MODEL
SWIGLU_LIMIT = 7.0
SWIGLU_ALPHA = 1.702
MOE_BLOCK = 128
Q_BLOCK = 128
SLC_Q_BLOCK = 32
FORCE_SCORE = 1e4
LN_EPS = 1e-5
RMS_EPS = 1e-6
DEEPNORM_ALPHA = (2 * DEPTH) ** 0.25
DEEPNORM_BETA = (8 * DEPTH) ** -0.25
IN_SPLITS = (
    NSA_HEADS * HEAD_DIM,
    NSA_KV_HEADS * HEAD_DIM,
    NSA_KV_HEADS * HEAD_DIM,
    NSA_KV_HEADS * HEAD_DIM,
    NSA_KV_HEADS * HEAD_DIM,
    NSA_KV_HEADS * HEAD_DIM,
    NSA_KV_HEADS * HEAD_DIM,
    NSA_HEADS * 3,
    DSA_HEADS * HEAD_DIM,
    KV_LATENT,
    IDX_HEADS * IDX_DIM,
    IDX_DIM,
    IDX_HEADS,
)
IN_COLS = sum(IN_SPLITS)

kernel_name = 'hybrid_nsa_dsa_moe_deepnorm_block'

def layer_norm(x, g, b):
    xf = x.astype(jnp.float32)
    mu = jnp.mean(xf, -1, keepdims=True)
    var = jnp.mean(jnp.square(xf - mu), -1, keepdims=True)
    return ((xf - mu) * lax.rsqrt(var + LN_EPS) * g + b).astype(x.dtype)

def rms_norm(x, g):
    xf = x.astype(jnp.float32)
    return (xf * lax.rsqrt(jnp.mean(jnp.square(xf), -1, keepdims=True) + RMS_EPS) * g).astype(x.dtype)

def t5_bucket(dist):
    d = jnp.maximum(dist, 0)
    df = jnp.maximum(d, 1).astype(jnp.float32)
    large = BUCKET_EXACT + (jnp.log(df / BUCKET_EXACT) / math.log(BUCKET_MAX_DIST / BUCKET_EXACT)
                            * (N_BUCKETS - BUCKET_EXACT)).astype(jnp.int32)
    large = jnp.minimum(large, N_BUCKETS - 1)
    return jnp.where(d < BUCKET_EXACT, d, large)

def masked_softmax(logits, mask):
    l = jnp.where(mask, logits, -jnp.inf)
    m = jnp.max(l, -1, keepdims=True)
    m = jnp.where(jnp.isfinite(m), m, 0.0)
    e = jnp.where(mask, jnp.exp(l - m), 0.0)
    s = jnp.sum(e, -1, keepdims=True)
    return e / jnp.where(s > 0, s, 1.0)

def to_blocks(a, nb):
    return jnp.moveaxis(a.reshape(a.shape[0], nb, -1, *a.shape[2:]), 1, 0)

def from_blocks(o):
    o = jnp.moveaxis(o, 0, 1)
    return o.reshape(o.shape[0], -1, *o.shape[3:])

def cmp_block_index(S):
    n_c = (S - CMP_LEN) // CMP_STRIDE + 1
    return np.arange(n_c)[:, None] * CMP_STRIDE + np.arange(CMP_LEN)[None, :]

def cmp_to_slc_matrix(cmp_starts, n_slc):
    ss = np.arange(n_slc) * SLC_LEN
    ov = np.minimum(cmp_starts[:, None] + CMP_LEN, ss[None, :] + SLC_LEN) - np.maximum(cmp_starts[:, None], ss[None, :])
    return (np.clip(ov, 0, None) / CMP_STRIDE).astype(np.float32)

def compress_blocks(kv, blk_idx, pos, w1, w2):
    B, n_c = kv.shape[0], blk_idx.shape[0]
    blocks = kv[:, blk_idx] + pos[None, None, :, None, :]
    blocks = jnp.moveaxis(blocks, 3, 2).reshape(B, n_c, NSA_KV_HEADS, CMP_LEN * HEAD_DIM)
    return jax.nn.gelu(blocks @ w1) @ w2

def nsa_mixer(q, k_cmp, v_cmp, k_slc, v_slc, k_win, v_win, gates,
              cmp_k_pos, cmp_k_w1, cmp_k_w2, cmp_v_pos, cmp_v_w1, cmp_v_w2, tab):
    B, S = q.shape[:2]
    G, R, dh = NSA_KV_HEADS, NSA_REP, HEAD_DIM
    scale = dh ** -0.5
    q = q.reshape(B, S, G, R, dh)
    k_cmp, v_cmp, k_slc, v_slc, k_win, v_win = [a.reshape(B, S, G, dh) for a in (k_cmp, v_cmp, k_slc, v_slc, k_win, v_win)]
    tab = tab.reshape(N_BUCKETS, G, R)
    t = jnp.arange(S)

    blk_idx = cmp_block_index(S)
    kc = compress_blocks(k_cmp, blk_idx, cmp_k_pos, cmp_k_w1, cmp_k_w2)
    vc = compress_blocks(v_cmp, blk_idx, cmp_v_pos, cmp_v_w1, cmp_v_w2)
    dist_c = t[:, None] - jnp.asarray(blk_idx[:, -1])[None, :]
    bias_c = jnp.transpose(tab[t5_bucket(dist_c)], (2, 3, 0, 1))
    logits_c = jnp.einsum('bsgrd,bcgd->bgrsc', q, kc).astype(jnp.float32) * scale + bias_c
    p_c = masked_softmax(logits_c, dist_c >= 0)
    o_cmp = jnp.einsum('bgrsc,bcgd->bsgrd', p_c.astype(vc.dtype), vc)

    n_slc = S // SLC_LEN
    n_sel = min(SLC_COUNT, n_slc)
    imp = jnp.einsum('bgrsc,cj->bgsj', p_c, jnp.asarray(cmp_to_slc_matrix(blk_idx[:, 0], n_slc)))
    j = jnp.arange(n_slc)[None, :]
    tb = (t // SLC_LEN)[:, None]
    valid = j <= tb
    forced = valid & ((j == 0) | (j >= tb - 1))
    score = jnp.where(valid, jnp.where(forced, FORCE_SCORE, imp), -jnp.inf)
    top_sc, top_idx = lax.top_k(score, n_sel)
    top_ok = top_sc > -jnp.inf
    kb = k_slc.reshape(B, n_slc, SLC_LEN, G, dh).transpose(0, 3, 1, 2, 4)
    vb = v_slc.reshape(B, n_slc, SLC_LEN, G, dh).transpose(0, 3, 1, 2, 4)
    tab_g = jnp.transpose(tab, (1, 0, 2))
    b_ix = jnp.arange(B)[:, None, None, None]
    g_ix = jnp.arange(G)[None, :, None, None]
    nqs = S // SLC_Q_BLOCK

    def slc_block(args):
        qi, qb, ib, okb = args
        tq = qi * SLC_Q_BLOCK + jnp.arange(SLC_Q_BLOCK)
        ks = kb[b_ix, g_ix, ib]
        vs = vb[b_ix, g_ix, ib]
        pos = ib[..., None] * SLC_LEN + jnp.arange(SLC_LEN)
        dist = tq[None, None, :, None, None] - pos
        mask = (okb[..., None] & (dist >= 0)).reshape(B, G, 1, SLC_Q_BLOCK, n_sel * SLC_LEN)
        bias = jnp.moveaxis(tab_g[g_ix[..., None], t5_bucket(dist)], -1, 2)
        logits = jnp.einsum('bqgrd,bgqnud->bgrqnu', qb, ks).astype(jnp.float32) * scale + bias
        p = masked_softmax(logits.reshape(B, G, R, SLC_Q_BLOCK, n_sel * SLC_LEN), mask)
        return jnp.einsum('bgrqn,bgqnd->bqgrd', p.astype(vs.dtype),
                          vs.reshape(B, G, SLC_Q_BLOCK, n_sel * SLC_LEN, dh))

    idx_blocks = jnp.moveaxis(top_idx.reshape(B, G, nqs, SLC_Q_BLOCK, n_sel), 2, 0)
    ok_blocks = jnp.moveaxis(top_ok.reshape(B, G, nqs, SLC_Q_BLOCK, n_sel), 2, 0)
    o_slc = from_blocks(lax.map(slc_block, (jnp.arange(nqs), to_blocks(q, nqs), idx_blocks, ok_blocks)))

    kp = jnp.pad(k_win, ((0, 0), (WINDOW, 0), (0, 0), (0, 0)))
    vp = jnp.pad(v_win, ((0, 0), (WINDOW, 0), (0, 0), (0, 0)))
    span = WINDOW + Q_BLOCK
    nqw = S // Q_BLOCK

    def win_block(args):
        qi, qb = args
        start = qi * Q_BLOCK
        kw = lax.dynamic_slice_in_dim(kp, start, span, axis=1)
        vw = lax.dynamic_slice_in_dim(vp, start, span, axis=1)
        tq = start + jnp.arange(Q_BLOCK)
        pos = start - WINDOW + jnp.arange(span)
        dist = tq[:, None] - pos[None, :]
        mask = (dist >= 0) & (dist < WINDOW) & (pos[None, :] >= 0)
        bias = jnp.transpose(tab[t5_bucket(dist)], (2, 3, 0, 1))
        logits = jnp.einsum('bqgrd,bkgd->bgrqk', qb, kw).astype(jnp.float32) * scale + bias
        p = masked_softmax(logits, mask)
        return jnp.einsum('bgrqk,bkgd->bqgrd', p.astype(vw.dtype), vw)

    o_win = from_blocks(lax.map(win_block, (jnp.arange(nqw), to_blocks(q, nqw))))

    g = jax.nn.sigmoid(gates.astype(jnp.float32)).reshape(B, S, G, R, 3).astype(q.dtype)
    o = g[..., 0:1] * o_cmp + g[..., 1:2] * o_slc + g[..., 2:3] * o_win
    return o.reshape(B, S, NSA_HEADS * dh)

def dsa_mixer(q, c_kv, q_idx, k_idx, w_idx, ckv_gain, kidx_gain, kidx_bias, w_uk, w_uv, tab):
    B, S = q.shape[:2]
    scale = HEAD_DIM ** -0.5
    q = q.reshape(B, S, DSA_HEADS, HEAD_DIM)
    ckv = rms_norm(c_kv, ckv_gain)
    q_abs = jnp.einsum('bshd,hcd->bshc', q, w_uk)
    qi = q_idx.reshape(B, S, IDX_HEADS, IDX_DIM)
    ki = layer_norm(k_idx, kidx_gain, kidx_bias)
    wi = w_idx * (IDX_HEADS ** -0.5 * IDX_DIM ** -0.5)
    k_top = min(IDX_TOPK_MAX, S // 4)
    nq = S // Q_BLOCK
    s_pos = jnp.arange(S)
    b_ix = jnp.arange(B)[:, None, None]

    def dsa_block(args):
        n, qab, qib, wib = args
        tq = n * Q_BLOCK + jnp.arange(Q_BLOCK)
        rel = jax.nn.relu(jnp.einsum('bqhd,bsd->bqhs', qib, ki).astype(jnp.float32))
        score = jnp.einsum('bqhs,bqh->bqs', rel, wib.astype(jnp.float32))
        score = jnp.where(s_pos[None, :] <= tq[:, None], score, -jnp.inf)
        top_sc, top_idx = lax.top_k(score, k_top)
        ok = top_sc > -jnp.inf
        cs = ckv[b_ix, top_idx]
        bias = jnp.moveaxis(tab[t5_bucket(tq[None, :, None] - top_idx)], -1, 1)
        logits = jnp.einsum('bqhc,bqkc->bhqk', qab, cs).astype(jnp.float32) * scale + bias
        p = masked_softmax(logits, ok[:, None])
        oc = jnp.einsum('bhqk,bqkc->bqhc', p.astype(cs.dtype), cs)
        return jnp.einsum('bqhc,hcd->bqhd', oc, w_uv)

    o = from_blocks(lax.map(dsa_block, (jnp.arange(nq), to_blocks(q_abs, nq), to_blocks(qi, nq), to_blocks(wi, nq))))
    return o.reshape(B, S, DSA_HEADS * HEAD_DIM)

def moe_ffn(h, w_router, b_router, w_gate, b_gate, w_up, b_up, w_down, b_down):
    T, D = h.shape
    logits = (h @ w_router + b_router).astype(jnp.float32)
    top_val, top_exp = lax.top_k(logits, TOP_K)
    gate_w = jax.nn.softmax(top_val, axis=-1)
    n_assign = T * TOP_K
    flat_e = top_exp.reshape(-1)
    order = jnp.argsort(flat_e)
    sorted_e = flat_e[order]
    sorted_tok = (jnp.arange(n_assign) // TOP_K)[order]
    sorted_w = gate_w.reshape(-1)[order]
    counts = jnp.bincount(flat_e, length=N_EXPERTS)
    padded = (counts + MOE_BLOCK - 1) // MOE_BLOCK * MOE_BLOCK
    pad_end = jnp.cumsum(padded)
    pad_start = pad_end - padded
    grp_start = jnp.cumsum(counts) - counts
    dest = pad_start[sorted_e] + jnp.arange(n_assign) - grp_start[sorted_e]
    n_rows = -(-n_assign // MOE_BLOCK) * MOE_BLOCK + N_EXPERTS * MOE_BLOCK
    n_blocks = n_rows // MOE_BLOCK
    x_pad = jnp.zeros((n_rows, D), h.dtype).at[dest].set(h[sorted_tok])
    blk_e = jnp.minimum(jnp.searchsorted(pad_end, jnp.arange(n_blocks) * MOE_BLOCK, side='right'), N_EXPERTS - 1)

    def expert_block(args):
        xb, e = args
        gt = jnp.minimum(xb @ w_gate[e] + b_gate[e], SWIGLU_LIMIT)
        up = jnp.clip(xb @ w_up[e] + b_up[e], -SWIGLU_LIMIT, SWIGLU_LIMIT)
        return (gt * jax.nn.sigmoid(SWIGLU_ALPHA * gt) * (up + 1.0)) @ w_down[e] + b_down[e]

    y_pad = lax.map(expert_block, (x_pad.reshape(n_blocks, MOE_BLOCK, D), blk_e)).reshape(n_rows, D)
    y = jax.ops.segment_sum(y_pad[dest] * sorted_w[:, None].astype(h.dtype), sorted_tok, num_segments=T)
    return y.astype(h.dtype)

def setup_inputs(seed: int = 0) -> dict:
    key = jax.random.key(seed)
    ks = jax.random.split(key, 40)
    L, D, E, F = DEPTH, D_MODEL, N_EXPERTS, D_EXPERT

    def nrm(k, shape, s):
        return jax.random.normal(k, shape, jnp.float32) * s

    return {
        'x': nrm(ks[0], (BATCH, SEQ, D), 1.0),
        'c': nrm(ks[1], (BATCH, D), 1.0),
        'w_ada': nrm(ks[2], (L, D, 6 * D), 0.2 * D ** -0.5),
        'b_ada': nrm(ks[3], (L, 6 * D), 0.01),
        'w_in': nrm(ks[4], (L, D, IN_COLS), D ** -0.5),
        'cmp_k_pos': nrm(ks[5], (L, CMP_LEN, HEAD_DIM), 0.1),
        'cmp_k_w1': nrm(ks[6], (L, CMP_LEN * HEAD_DIM, CMP_HIDDEN), (CMP_LEN * HEAD_DIM) ** -0.5),
        'cmp_k_w2': nrm(ks[7], (L, CMP_HIDDEN, HEAD_DIM), CMP_HIDDEN ** -0.5),
        'cmp_v_pos': nrm(ks[8], (L, CMP_LEN, HEAD_DIM), 0.1),
        'cmp_v_w1': nrm(ks[9], (L, CMP_LEN * HEAD_DIM, CMP_HIDDEN), (CMP_LEN * HEAD_DIM) ** -0.5),
        'cmp_v_w2': nrm(ks[10], (L, CMP_HIDDEN, HEAD_DIM), CMP_HIDDEN ** -0.5),
        'ckv_gain': 1.0 + nrm(ks[11], (L, KV_LATENT), 0.02),
        'kidx_gain': 1.0 + nrm(ks[12], (L, IDX_DIM), 0.02),
        'kidx_bias': nrm(ks[13], (L, IDX_DIM), 0.02),
        'w_uk': nrm(ks[14], (L, DSA_HEADS, KV_LATENT, HEAD_DIM), HEAD_DIM ** -0.5),
        'w_uv': nrm(ks[15], (L, DSA_HEADS, KV_LATENT, HEAD_DIM), KV_LATENT ** -0.5),
        'nsa_out_gain': 1.0 + nrm(ks[16], (L, NSA_HEADS * HEAD_DIM), 0.02),
        'dsa_out_gain': 1.0 + nrm(ks[17], (L, DSA_HEADS * HEAD_DIM), 0.02),
        'rel_bias': nrm(ks[18], (N_BUCKETS, N_HEADS_TOTAL), 0.5),
        'w_out': nrm(ks[19], (L, MIX_WIDTH, D), DEEPNORM_BETA * MIX_WIDTH ** -0.5),
        'ln1_gain': 1.0 + nrm(ks[20], (L, D), 0.02),
        'ln1_bias': nrm(ks[21], (L, D), 0.02),
        'w_router': nrm(ks[22], (L, D, E), D ** -0.5),
        'b_router': nrm(ks[23], (L, E), 0.01),
        'w_gate': nrm(ks[24], (L, E, D, F), D ** -0.5),
        'b_gate': nrm(ks[25], (L, E, F), 0.01),
        'w_up': nrm(ks[26], (L, E, D, F), D ** -0.5),
        'b_up': nrm(ks[27], (L, E, F), 0.01),
        'w_down': nrm(ks[28], (L, E, F, D), DEEPNORM_BETA * F ** -0.5),
        'b_down': nrm(ks[29], (L, E, D), 0.01),
        'ln2_gain': 1.0 + nrm(ks[30], (L, D), 0.02),
        'ln2_bias': nrm(ks[31], (L, D), 0.02),
    }

def reference(x, c, w_ada, b_ada, w_in, cmp_k_pos, cmp_k_w1, cmp_k_w2, cmp_v_pos, cmp_v_w1, cmp_v_w2,
              ckv_gain, kidx_gain, kidx_bias, w_uk, w_uv, nsa_out_gain, dsa_out_gain, rel_bias, w_out,
              ln1_gain, ln1_bias, w_router, b_router, w_gate, b_gate, w_up, b_up, w_down, b_down,
              ln2_gain, ln2_bias):
    B, S, D = x.shape
    split_points = [int(p) for p in np.cumsum(IN_SPLITS)[:-1]]
    for l in range(DEPTH):
        ada = jax.nn.silu(c) @ w_ada[l] + b_ada[l]
        sh1, sc1, g1, sh2, sc2, g2 = [a[:, None, :] for a in jnp.split(ada, 6, axis=-1)]

        h = x * (1.0 + sc1) + sh1
        cols = jnp.split(h @ w_in[l], split_points, axis=-1)
        (q_n, kc_n, vc_n, ks_n, vs_n, kw_n, vw_n, gate_n, q_d, ckv_d, qi_d, ki_d, wi_d) = cols
        o_nsa = nsa_mixer(q_n, kc_n, vc_n, ks_n, vs_n, kw_n, vw_n, gate_n,
                          cmp_k_pos[l], cmp_k_w1[l], cmp_k_w2[l], cmp_v_pos[l], cmp_v_w1[l], cmp_v_w2[l],
                          rel_bias[:, :NSA_HEADS])
        o_dsa = dsa_mixer(q_d, ckv_d, qi_d, ki_d, wi_d, ckv_gain[l], kidx_gain[l], kidx_bias[l],
                          w_uk[l], w_uv[l], rel_bias[:, NSA_HEADS:])
        mix = jnp.concatenate([rms_norm(o_nsa, nsa_out_gain[l]), rms_norm(o_dsa, dsa_out_gain[l])], axis=-1)
        y = mix @ w_out[l]
        x = layer_norm(DEEPNORM_ALPHA * x + (1.0 + g1) * y, ln1_gain[l], ln1_bias[l])

        h = x * (1.0 + sc2) + sh2
        y = moe_ffn(h.reshape(B * S, D), w_router[l], b_router[l], w_gate[l], b_gate[l],
                    w_up[l], b_up[l], w_down[l], b_down[l]).reshape(B, S, D)
        x = layer_norm(DEEPNORM_ALPHA * x + (1.0 + g2) * y, ln2_gain[l], ln2_bias[l])
    return x


_drawn_inputs = setup_inputs


def setup_inputs(seed=0):
    import zlib

    import numpy as np

    out = dict(_drawn_inputs(seed))
    spreads = {}
    factors = {'cmp_k_pos': 4.949,
     'ckv_gain': 3.015,
     'nsa_out_gain': 3.43,
     'dsa_out_gain': 3.903,
     'b_router': 3.682,
     'b_gate': 22.627,
     'b_up': 33.13,
     'b_down': 8.0,
     'ln2_gain': 7.693,
     'ln2_bias': 8.038}
    for name, (base, spread) in spreads.items():
        noise = np.random.default_rng([zlib.crc32(name.encode()), seed]).standard_normal(out[name].shape)
        drawn = base * np.exp(spread * noise) if base else spread * noise
        out[name] = jnp.asarray(drawn.astype(out[name].dtype))
    for name, factor in factors.items():
        out[name] = (out[name] * factor).astype(out[name].dtype)
    return out
```

```python
import math
from contextlib import ExitStack

import concourse.bass as bass
import numpy as np
from concourse import mybir

T = 512
D = 1024
P = 128
QT = T // P
KC = D // P
DH = 64
NH = 8
NG = 2
CMP_LEN, CMP_STRIDE = 32, 16
NCMP = (T - CMP_LEN) // CMP_STRIDE + 1
LC = CMP_LEN * DH // P
FH = 256
TOPK_KEYS = min(256, T // 4)
NE = 32
TOPK_EXP = 4
BIG = 1e30
ALPHA = 2 ** 0.25
N_BUCKETS = 32
EW = 1024
MW = 896
IN_COLS = 2528

W_IN_MOVES = [(512, 512, 384), (1024, 896, 128), (896, 2048, 128), (1152, 2176, 152),
              (1816, 2328, 128), (2456, 2456, 72), (1944, 1536, 512)]
W_IN_MOVES += [(256 * g + 64 * j, 128 * j + 64 * g, 64) for j in range(4) for g in range(2)]
W_IN_MOVES += [(1304, 1024, 512)]
QN, KCC, VCC, KSC, KWC, QD, QI, NAT = 0, 512, 640, 768, 896, 1024, 1536, 2048
NATW = 480
N_VS, N_VW, N_GATE, N_CKV, N_KI, N_WI = 0, 128, 256, 280, 408, 472

SLC, WIN, DSA = 0, 1, 2
UNITS = [(b, h, q) for h in range(NH) for b in (SLC, WIN) for q in range(QT)]
UNITS += [(DSA, h, q) for h in range(NH) for q in range(QT)]
NU = len(UNITS)

C_ID, C_TRI, C_IOTA, C_CMASK, C_CAUS, C_TV, C_DUM, C_NDUM, C_W = 0, 128, 256, 384, 508, 636, 640, 641, 642


def build_layer(nc, a, out):
    f32, bf16, i32, u32 = mybir.dt.float32, mybir.dt.bfloat16, mybir.dt.int32, mybir.dt.uint32
    ALU, ACT, AX = mybir.AluOpType, mybir.ActivationFunctionType, mybir.AxisListType
    ds = bass.ds
    ctx = ExitStack()
    with ctx:
        def sb(name, shape, dt=f32):
            return ctx.enter_context(nc.sbuf_tensor(name, shape, dt))

        def sem(name):
            return ctx.enter_context(nc.semaphore(name))

        ring = sb("ring", [P, 24, D])
        att = sb("att", [P, 16384])
        hT = sb("hT", [P, KC, T])
        pa = sb("pa", [P, 4096])
        ringf = ring[:, :, :].rearrange("p a b -> p (a b)")
        hTf = hT[:, :, :].rearrange("p a b -> p (a b)")
        w_in = ringf[:, 0:KC * IN_COLS].rearrange("p (k n) -> p k n", k=KC)
        w1 = ringf[:, 0:8192].rearrange("p (s l f) -> p s l f", s=2, l=LC)
        ada1 = att[:, :].rearrange("p (k n) -> p k n", k=KC)

        def part(first, *shape):
            n = 1
            for s in shape:
                n *= s
            v = att[:, first:first + n]
            if len(shape) == 2:
                v = v.rearrange("p (a b) -> p a b", a=shape[0])
            return v
        qnT = part(0, 4, T)
        kcT, vcT, ksT, kwT = (part(2048 + 512 * n, T) for n in range(4))
        qdT = part(4096, 4, T)
        qiT = part(6144, 4, T)
        nat = part(8192, QT, NATW)
        kdT = part(10112, 4, T)
        vd = part(12160, QT, T)
        ckvT = part(14208, T)
        kiT = part(14720, T)
        score = part(15232, T)
        work = part(15744, T)
        o = hTf.rearrange("p (q n) -> p q n", q=QT)
        xn = pa[:, :].rearrange("p (q n) -> p q n", q=QT)
        Sb = pa[:, 0:2048].rearrange("p (u n) -> p u n", u=4)
        PTs = pa[:, 2048:4096].rearrange("p (u n) -> p u n", u=4)
        X = pa[:, 0:2048].rearrange("p (s g t) -> p s g t", s=2, g=NG)
        blk = pa[:, 2048:2048 + 2 * LC * NG * NCMP].rearrange("p (s l g c) -> p s l g c", s=2, l=LC, g=NG)
        mixT = pa[:, :].rearrange("p (k t) -> p k t", k=KC)

        cst = sb("cst", [P, C_W])
        ident = cst[:, C_ID:C_ID + P]
        identb = sb("identb", [P, P], bf16)
        master = sb("master", [P, 2, MW])
        onehot = master[0:N_BUCKETS + 1, 0:2, :].rearrange("p a b -> p (a b)")[:, 0:EW]
        small = sb("small", [P, 600])
        cT, siluc = small[:, 0:8], small[:, 8:16]
        badaT, adaT = small[:, 16:32], small[:, 32:48]
        ckvg, kig, kib = small[:, 48:49], small[:, 49:50], small[:, 50:51]
        og = small[:, 52:60]
        tab = small[:, 60:76]
        pos2 = small[:, 76:108].rearrange("p (s l) -> p s l", s=2)
        gsig = small[:, 108:204].rearrange("p (q n) -> p q n", q=QT)
        wis = small[:, 204:236].rearrange("p (q n) -> p q n", q=QT)
        st = small[:, 236:260].rearrange("p (q n) -> p q n", q=QT)
        mv = small[:, 260:268].rearrange("p (q n) -> p q n", q=QT)
        ss4, rs4, rk4 = small[:, 268:272], small[:, 272:276], small[:, 276:280]
        usum, umin = small[:, 280:376], small[:, 376:472]
        rsum = small[:, 472:568]
        max8 = small[:, 568:576]
        cnt, need = small[:, 576:577], small[:, 577:578]
        ssq, rr8 = small[:, 580:588], small[:, 588:596]
        kin = work.rearrange("p (q n) -> p q n", q=QT)
        w2 = sb("w2", [P, 2, 2, DH])
        wukv = ringf[:, 20480:21504].rearrange("p (s h d) -> p s h d", s=2, h=NH)
        sel_s = ringf[:, 21504:23040].rearrange("p (q t) -> p q t", q=3)
        E_sb = ringf[0:16, 21504:21504 + EW]
        selm = ringf[:, 23040:23808].bitcast(bf16).rearrange("p (q t) -> p q t", q=3)
        PcT = ringf[0:NCMP, 23808:24320]
        cone = ringf[:, 24320:24576].bitcast(bf16)
        gelu = sb("gelu", [P, 2, 2, 2 * NCMP])
        gt1 = sb("gt1", [P, 2, 2, 2 * NCMP])
        kcmpT = sb("kcmpT", [P, NCMP])
        vcmp = sb("vcmp", [NCMP, NG, DH])
        Pc = part(16256, QT, NCMP)
        cm4 = sb("cm4", [P, 4, QT])

        bank = [ctx.enter_context(nc.psum_tensor(f"bank{n}", [P, 512], f32)) for n in range(8)]

        XB = [bank[n] for n in (2, 3, 4, 5, 6, 0, 1, 2)]
        e_d = nc.dram_tensor("bias_by_distance", (16, EW), f32).ap()

        w_out = ringf[:, 8192:16384].rearrange("p (k n) -> p k n", k=KC)
        ada_ring = [ringf[:, n * 4096:(n + 1) * 4096].rearrange("p (k n) -> p k n", k=KC) for n in range(2)]
        ada_att = [att[:, 8192 + n * 4096:8192 + (n + 1) * 4096].rearrange("p (k n) -> p k n", k=KC) for n in range(2)]
        ada_half = ada_ring + ada_att + ada_ring + ada_att
        rows = [att[:, n * D:(n + 1) * D] for n in range(8)]
        g1r, sc2r, sh2r, ln1g, ln1b, g2r, ln2g, ln2b = rows
        b_f32 = ringf[0:NE, 8192:8192 + 3 * D].rearrange("e (m n) -> e m n", m=3)
        b_part = ringf[0:NE, 11264:11264 + 9 * D // 2].bitcast(bf16).rearrange("e (s m n) -> e s m n", s=3, m=3)
        x1 = o
        yt = ringf[:, 16384:18432].rearrange("p (u n) -> p u n", u=2)
        h2 = ringf[:, 18432:20480].rearrange("p (u n) -> p u n", u=2)
        h2T = ringf[:, 20480:21504].rearrange("p (k t) -> p k t", k=KC)
        zero = ringf[:, 21504:22528]
        w_rt = ringf[:, 22528:22784].rearrange("p (k e) -> p k e", k=KC)
        b_rt = ringf[:, 22784:22816]
        ms = master[:, :, :].rearrange("p a b -> p (a b)")
        TG = ms[:, 0:396].rearrange("p (q e n) -> p q e n", q=QT, n=3)
        posr = ms[:, 400:928].rearrange("p (q n) -> p q n", q=QT)
        lg, sel, eq4, cum4, ex4 = (ms[:, 928 + 128 * n:1056 + 128 * n].rearrange("p (q e) -> p q e", q=QT) for n in range(5))
        selb = ms[:, 1568:1632].bitcast(bf16).rearrange("p (q e) -> p q e", q=QT)
        m8 = ms[:, 1632:1664].rearrange("p (q n) -> p q n", q=QT)
        rsm = ms[:, 1664:1696].rearrange("p (n q) -> p n q", q=QT)
        rounds_i = ms[:, 1696:1697].bitcast(i32)
        most = ms[:, 1697:1700]
        slot_in = ms[:, 1700:1708].rearrange("p (u n) -> p u n", u=2)
        idx_g = ms[:, 1708:1710].bitcast(u32)
        idx_s = ms[:, 1710:1712].bitcast(u32)
        slot_t = ms[:, 1712:1714]
        lnst = ms[:, 1714:1762].rearrange("p (q n) -> p q n", q=QT)
        lnmv = ms[:, 1762:1770].rearrange("p (q n) -> p q n", q=QT)
        lnr = ms[:, 1770:1778].rearrange("p (n q) -> p n q", q=QT)
        trib = identb

        def att_k(n):
            return att[:, n * D:(n + 1) * D]
        bp = [att[:, 1536 * n:1536 * (n + 1)].bitcast(bf16) for n in range(2)]
        onesb = w2[:, :, :, :].rearrange("p a b c -> p (a b c)")[:, 0:64].bitcast(bf16)
        xg = [att_k(8), att_k(9)]
        hTe = [att_k(10 + n).rearrange("p (k t) -> p k t", k=KC) for n in range(2)]
        gts, sgm, ucl, prod = att_k(12), att_k(13), att_k(14), att_k(15)
        actT = pa[:, 0:D].rearrange("p (k t) -> p k t", k=KC)
        yb = [pa[:, D:2 * D], pa[:, 2 * D:3 * D]]
        OH = pa[:, 3072:3584].rearrange("p (q n) -> p q n", q=QT)
        acc = ringf[:, 0:4096].rearrange("p (q n) -> p q n", q=QT)
        ft = ringf[:, 4096:8192].rearrange("p (q n) -> p q n", q=QT)

        bparts_d = nc.dram_tensor("bias_parts", (NE, 3, 3 * D), bf16).ap()
        h2_d = nc.dram_tensor("moe_input", (T, D), f32).ap()
        acc_d = nc.dram_tensor("moe_output", (T + P, D), f32).ap()

        loads = {}

        def loaded(name):
            if name not in loads:
                loads[name] = sem("ld_" + name)
            return loads[name]
        chain_s = {k: sem("own_" + k) for k in ("dve", "act", "pool")}
        s_bias = sem("bias_table_ready")
        s_bias_sb = sem("bias_table_in_sbuf")
        s_silu = sem("silu_ready")
        s_xT = sem("xT_ready")
        s_ada = sem("ada_ready")
        s_adaT = sem("ada_columns_ready")
        s_hT = sem("hT_ready")
        s_proj = sem("proj_done")
        s_pev = [sem("proj_evac_dve"), sem("proj_evac_act")]
        s_nat = sem("norms_ready")
        s_sqrt = sem("sqrt_done")
        s_kvar = sem("variances_ready")
        s_ctr = sem("ckv_ki_transposed")
        s_cev = sem("ckv_ki_in_sbuf")
        s_kv = sem("dsa_kv_done")
        s_kvev = sem("dsa_kv_in_sbuf")
        s_X = sem("shifted_ready")
        s_blk = sem("blocks_ready")
        s_hid = sem("hidden_ready")
        s_gel = sem("gelu_ready")
        s_ga = sem("gelu_arg_ready")
        s_gt = sem("gelu_tanh_ready")
        s_cmp = sem("compressed_ready")
        s_cmpev = sem("compressed_in_sbuf")
        s_is = sem("index_scores_done")
        s_relu = sem("relu_ready")
        s_isc = sem("index_score_used")
        s_S = sem("logits_done")
        s_ttr = sem("biased_ready")
        s_exp = sem("exp_ready")
        s_T = sem("probs_transposed")
        s_Tev = sem("probsT_in_sbuf")
        s_PV = sem("pv_done")
        s_oev = sem("o_updated")
        s_sel = sem("selection_ready")
        s_cS, s_cSub, s_cExp, s_cN = sem("cmp_logits"), sem("cmp_shifted"), sem("cmp_exp"), sem("cmp_probs")
        s_cT, s_cTev, s_cPV, s_cO = sem("cmp_T"), sem("cmp_T_in_sbuf"), sem("cmp_pv"), sem("cmp_added")
        s_hTa, s_gsig, s_tab, s_idb = sem("hT_ready_act"), sem("gates_ready"), sem("table_row_ready"), sem("ident_bf16_ready")
        sem_e = sem("own_dve_experts")

        s_row, s_rowev = sem("ada_row_done"), sem("ada_row_in_sbuf")
        s_ssq, s_ms, s_rt, s_osc = sem("squares_summed"), sem("mean_square"), sem("root_ready"), sem("o_scaled")
        s_mT, s_mTev = sem("mix_transposed"), [sem("mixT_dve"), sem("mixT_act")]
        s_y, s_yrd = sem("w_out_done"), sem("y_used")
        s_lv, s_lr, s_xh, s_h2, s_h2st = sem("ln_var"), sem("ln_root"), sem("xhat_ready"), sem("h2_ready"), [sem(f"h2_stored{n}") for n in range(2)]
        s_ab, s_x1, s_xhfree = sem("ln_rows_ready"), sem("x1_ready"), sem("xhat_used")
        s_rT, s_rTev, s_rl, s_rlv, s_rex, s_rnm = sem("h2_transposed"), sem("h2T_in_sbuf"), sem("router_logits"), sem("router_logits_used"), sem("router_exp"), sem("router_max")
        s_selb, s_trib, s_pos, s_tables = sem("selected_ready"), sem("tri_ready"), sem("positions_done"), sem("tables_ready")
        s_bsp, s_bst, s_zero, s_zst = sem("bias_split"), sem("bias_parts_stored"), sem("zero_ready"), sem("moe_output_zeroed")
        s_used = sem("ring_slots_used")
        s_w = [sem(f"slot{n}_loaded") for n in range(12)]
        s_bp = [sem(f"bias_parts{n}_loaded") for n in range(2)]
        s_oh, s_rtm, s_idx = sem("one_hot_ready"), sem("slots_done"), sem("slot_indices_ready")
        s_g = [sem(f"gathered{n}") for n in range(2)]
        s_tx, s_xe = sem("rows_transposed"), [sem("rowsT_dve"), sem("rowsT_act")]
        s_gdr, s_sig, s_uh, s_udr, s_act = sem("gate_read"), sem("sigmoid_ready"), sem("up_half_done"), sem("up_read"), sem("act_ready")
        s_ta, s_at, s_yb, s_sc = sem("act_transposed"), sem("actT_in_sbuf"), sem("y_ready"), sem("scattered")
        s_al, s_fv, s_fr, s_fh, s_fo, s_out = sem("moe_output_loaded"), sem("final_var"), sem("final_root"), sem("final_xhat"), sem("final_ready"), sem("stored")

        s_bpz = sem("bias_buffers_zeroed")
        s_past = sem("pool_past_waits")

        proj = [(True, KCC, kcT), (True, VCC, vcT)] + [(False, q, nat[:, q, :]) for q in range(QT)]
        proj += [(True, KSC, ksT), (True, KWC, kwT)]
        proj += [(True, QI + P * j, qiT[:, j, :]) for j in range(4)]
        proj += [(True, QN + P * j, qnT[:, j, :]) for j in range(4)]
        proj += [(True, QD + P * j, qdT[:, j, :]) for j in range(4)]
        NPJ = len(proj)

        def last_unit(m):
            return 8 * m + 7 if m < NH else 64 + 4 * (m - NH) + 3

        def pj_scale(i):
            return -0.125 if (i >= 12) else None

        def pj_wait(eng, i):
            eng.wait_ge(s_pev[i % 2], i // 2 + 1)

        blocks = ExitStack()
        block = blocks.enter_context(nc.Block())

        @block.sync
        def _(sp):
            def load(name, dst, src):
                sp.dma_start(dst, src).then_inc(loaded(name), 16)
            def row_load(n, src):
                load(f"rows{n // 4}", rows[n], src.to_broadcast([P, D]))

            def ada_load(n):
                c0 = (2, 2, 4, 4, 3, 3, 5, 5)[n] * D + (n % 2) * 512
                load(f"ada{n // 2}", ada_half[n], a["w_ada"][0, :, c0:c0 + 512].rearrange("(k p) n -> p k n", p=P))
            load("cst", cst[:, :], a["k_cst"])
            load("onehot", onehot, a["k_onehot"])
            load("tab", tab[0:N_BUCKETS, :], a["rel_bias"])
            with nc.allow_non_contiguous_dma(reason="small vectors with features on partitions"):
                load("c", cT, a["c"].rearrange("b (k p) -> p (b k)", p=P))
                load("bada", badaT, a["b_ada"][:, 0:2 * D].rearrange("b (k p) -> p (b k)", p=P))
            load("x", xn, a["x"].rearrange("b (q p) n -> p (b q) n", p=P))
            for half in range(2):
                load(f"ada1_{half}", ada1[:, :, half * D:(half + 1) * D],
                     a["w_ada"][0, :, half * D:(half + 1) * D].rearrange("(k p) n -> p k n", p=P))
            with nc.allow_non_contiguous_dma(reason="small vectors with features on partitions"):
                for s, n in enumerate(("cmp_k_pos", "cmp_v_pos")):
                    load("small", pos2[:, s, :], a[n][0].rearrange("(l p2) d -> (p2 d) l", p2=2))
                load("small", ckvg, a["ckv_gain"].rearrange("a p -> p a"))
                for half in range(2):
                    hs = slice(half * DH, (half + 1) * DH)
                    load("small", kig[hs], a["kidx_gain"].rearrange("a p -> p a"))
                    load("small", kib[hs], a["kidx_bias"].rearrange("a p -> p a"))
                load("small", og[:, 0:4], a["nsa_out_gain"].rearrange("a (k p) -> p (a k)", p=P))
                load("small", og[:, 4:8], a["dsa_out_gain"].rearrange("a (k p) -> p (a k)", p=P))
            for s, n in enumerate(("w_uk", "w_uv")):
                load("small", wukv[:, s], a[n][0].rearrange("h c d -> c h d"))
            for s, n in enumerate(("cmp_k_w2", "cmp_v_w2")):
                load("small", w2[:, s], a[n][0].rearrange("(f p) d -> p f d", p=P))
            for src, dst, w in W_IN_MOVES:
                load("w_in", w_in[:, :, dst:dst + w],
                     a["w_in"][0, :, src:src + w].rearrange("(k p) n -> p k n", p=P))
            sp.wait_ge(s_bias_sb, 1)
            load("e_d", e_d, E_sb[:, :])
            sp.wait_ge(loaded("e_d"), 16)
            pj_wait(sp, 0)
            pj_wait(sp, 1)
            for s, src in enumerate((kcT, vcT)):
                for g in range(NG):
                    for lp in range(2):
                        sp.dma_start(X[lp * DH:(lp + 1) * DH, s, g, 0:T - 1],
                                     src[g * DH:(g + 1) * DH, lp:T - 1 + lp]).then_inc(s_X, 16)
            sp.wait_ge(s_proj, NPJ)
            for s, n in enumerate(("cmp_k_w1", "cmp_v_w1")):
                load("w1", w1[:, s], a[n][0].rearrange("(l p) f -> p l f", p=P))
            for n, name in enumerate(("b_gate", "b_up", "b_down")):
                load("b_exp", b_f32[:, n, :], a[name][0])
            for m in range(16):
                if m == 4:
                    sp.wait_ge(s_hid, 1)
                    ada_load(0)
                    ada_load(1)
                    sp.wait_ge(s_bst, 16)
                    load("w_out", w_out, a["w_out"][0].rearrange("(k p) n -> p k n", p=P))
                if m == 12:
                    sp.wait_ge(s_S, 64)
                    row_load(0, a["b_ada"][:, 2 * D:3 * D])
                    row_load(1, a["b_ada"][:, 4 * D:5 * D])
                    row_load(2, a["b_ada"][:, 3 * D:4 * D])
                    row_load(3, a["ln1_gain"])
                if m >= 2:
                    sp.wait_ge(s_ttr, last_unit(m - 2) + 1)
                    sp.wait_ge(s_cSub, min(m - 1, NH))
                w = MW if m < 8 else T
                skewed = bass.AP(tensor=e_d.tensor, offset=m * EW + MW - w, ap=[[1, P], [1, w]])
                load(f"master{m % 2}", master[:, m % 2, 0:w], skewed)

            sp.wait_ge(s_S, NU)
            row_load(4, a["ln1_bias"])
            row_load(5, a["b_ada"][:, 5 * D:6 * D])
            row_load(6, a["ln2_gain"])
            row_load(7, a["ln2_bias"])
            sp.wait_ge(s_PV, NU)
            ada_load(2)
            ada_load(3)
            sp.wait_ge(s_oev, NU)
            load("w_rt", w_rt, a["w_router"][0].rearrange("(k p) n -> p k n", p=P))
            load("w_rt", b_rt, a["b_router"].to_broadcast([P, NE]))
            sp.wait_ge(s_row, 2)
            ada_load(4)
            ada_load(5)
            sp.wait_ge(s_mT, KC)
            load("x_again", x1, a["x"].rearrange("b (q p) n -> p (b q) n", p=P))
            sp.wait_ge(s_row, 4)
            ada_load(6)
            ada_load(7)
            for q in range(QT):
                sp.wait_ge(s_h2, q + 1)
                sp.dma_start(h2_d[q * P:(q + 1) * P, :], h2[:, q % 2, :]).then_inc(s_h2st[q % 2], 16)

            names = ("w_gate", "w_up", "w_down")

            def expert_loads(e, i, par, pair):
                for mx in range(3):
                    for j in range(4):
                        sp.wait_ge(s_used, i * 12 + (mx * 4 + j + 1))
                        if mx == 0 and j == 0:
                            sp.dma_start(bp[par][0:3, :], bparts_d[ds(e, 1), :, :].rearrange("a s n -> (a s) n")).then_inc(s_bp[par], 16)
                        sp.dma_start(ring[:, mx * 8 + 2 * j:mx * 8 + 2 * j + 2, :],
                                     a[names[mx]][0, ds(e, 1), j * 256:(j + 1) * 256, :].rearrange("a (c p) n -> p (a c) n", p=P)
                                     ).then_inc(s_w[mx * 4 + j], 16)
            sp.wait_ge(s_x1, QT)
            sp.wait_ge(s_tables, 1)
            sp.wait_ge(s_bpz, 1)
            sp.wait_ge(s_zst, 16 * (QT + 1))
            for n in range(2):
                sp.wait_ge(s_h2st[n], 32)
            n_rounds = sp.value_load(rounds_i[0:1, 0:1], min_val=1, max_val=QT)
            with sp.Fori(0, n_rounds) as rd:
                with sp.Fori(0, NE // 2) as ep:
                    for par in range(2):
                        expert_loads(ep * 2 + par, rd * NE + ep * 2 + par, par, rd * (NE // 2) + ep)
            for q in range(QT):
                sp.wait_ge(s_fo, q + 1)
                sp.dma_start(out[0, q * P:(q + 1) * P, :], ft[:, q, :]).then_inc(s_out, 16)
            sp.wait_ge(s_out, 16 * QT)

        @block.gpsimd
        def _(pool):
            pool.wait_ge(loaded("cst"), 16)
            nc.gpsimd.memset(cone, 1.0)
            nc.gpsimd.tensor_copy(identb[:, :], ident).then_inc(s_idb, 1)
            pool.wait_ge(s_X, 16 * 8)
            pool.wait_ge(loaded("small"), 16 * 13)
            for s in range(2):
                for g in range(NG):
                    base = X[:, s, g, :]
                    for lh in range(2):
                        v = base[:, 16 * lh:16 * lh + 496].rearrange("p (c l m) -> p l c m", l=8, m=2)[:, :, :, 0]
                        nc.gpsimd.tensor_tensor(
                            blk[:, s, 8 * lh:8 * lh + 8, g, :], v,
                            pos2[:, s, 8 * lh:8 * lh + 8].unsqueeze(2).to_broadcast([P, 8, NCMP]),
                            ALU.add).then_inc(s_blk, 1)

            pool.wait_ge(loaded("b_exp"), 48)
            own = [0]

            def link(ins):
                own[0] += 1
                ins.then_inc(chain_s["pool"], 1)
                pool.wait_ge(chain_s["pool"], own[0])
            for n in range(3):
                link(nc.gpsimd.tensor_copy(b_part[:, n, :, :], b_f32))
                if n < 2:
                    link(nc.gpsimd.tensor_tensor(b_f32, b_f32, b_part[:, n, :, :], ALU.subtract))
            pool.dma_start(bparts_d.rearrange("e s (m n) -> e s m n", m=3), b_part).then_inc(s_bst, 16)
            pool.wait_ge(s_S, NU)
            nc.gpsimd.memset(onesb, 1.0)
            nc.gpsimd.tensor_copy(trib[:, :], cst[:, C_TRI:C_TRI + P]).then_inc(s_trib, 1)
            pool.wait_ge(s_sel, 3)
            nc.gpsimd.memset(zero, 0.0).then_inc(s_zero, 1)
            pool.wait_ge(s_zero, 1)
            for n in range(QT + 1):
                pool.dma_start(acc_d[n * P:(n + 1) * P, :], zero).then_inc(s_zst, 16)
            pool.wait_ge(loaded("rows0"), 64)
            pool.wait_ge(loaded("rows1"), 64)
            pool.wait_ge(s_rowev, 6)
            link(nc.gpsimd.tensor_tensor(yt[:, 0, :], ln1b, sc2r, ALU.mult))
            nc.gpsimd.tensor_tensor(sc2r, sc2r, ln1g, ALU.mult)
            link(nc.gpsimd.tensor_tensor(sh2r, sh2r, yt[:, 0, :], ALU.add))
            nc.gpsimd.tensor_scalar(ln1g, ln1g, ALPHA, None, ALU.mult)
            nc.gpsimd.tensor_scalar(ln1b, ln1b, ALPHA, None, ALU.mult).then_inc(s_ab, 1)
            for q in range(QT):
                pool.wait_ge(s_xh, q + 1)
                pool.wait_ge(s_ab, 1)
                link(nc.gpsimd.tensor_tensor(x1[:, q, :], yt[:, q % 2, :], ln1g, ALU.mult))
                nc.gpsimd.tensor_tensor(x1[:, q, :], x1[:, q, :], ln1b, ALU.add).then_inc(s_x1, 1)

            pool.wait_ge(s_h2, QT)
            nc.gpsimd.memset(att[:, 0:3072], 0.0).then_inc(s_bpz, 1)

            def gather(par):
                pool.sem_inc(s_past, 1)
                pool.indirect_dma_start(xg[par], None, h2_d, bass.IndirectOffsetOnAxis(ap=idx_g[:, par:par + 1], axis=0)
                                        ).then_inc(s_g[par], 16)

            def scatter(par):
                pool.sem_inc(s_past, 1)
                pool.indirect_dma_start(acc_d, bass.IndirectOffsetOnAxis(ap=idx_s[:, par:par + 1], axis=0), yb[par], None,
                                        compute_op=ALU.add).then_inc(s_sc, 16)
            pool.wait_ge(s_h2st[0], 32)
            pool.wait_ge(s_h2st[1], 32)
            pool.wait_ge(s_zst, 16 * (QT + 1))
            pool.wait_ge(s_idx, 1)
            gather(0)
            n_rounds = pool.value_load(rounds_i[0:1, 0:1], min_val=1, max_val=QT)
            with pool.Fori(0, n_rounds) as rd:
                with pool.Fori(0, NE // 2) as ep:
                    for par in range(2):
                        i = rd * NE + ep * 2 + par
                        pool.wait_ge(s_idx, i + 2)
                        pool.wait_ge(s_tx, i)
                        gather(1 - par)
                        pool.wait_ge(s_yb, i * 2 + 2)
                        pool.wait_ge(s_sc, i * 16)
                        scatter(par)
            pool.wait_ge(s_sc, n_rounds * (NE * 16))
            pool.sem_inc(s_past, 1)
            pool.dma_start(acc, acc_d[0:T, :].rearrange("(q p) n -> p q n", p=P)).then_inc(s_al, 16)
            for q in (0, 2):
                pool.wait_ge(s_fh, q + 1)
                link(nc.gpsimd.tensor_tensor(ft[:, q, :], ft[:, q, :], ln2g, ALU.mult))
                pool.wait_ge(s_fo, q)
                nc.gpsimd.tensor_tensor(ft[:, q, :], ft[:, q, :], ln2b, ALU.add).then_inc(s_fo, 1)

        @block.tensor
        def _(pe):
            pe.wait_ge(loaded("onehot"), 16)
            pe.wait_ge(loaded("tab"), 16)
            pe.wait_ge(s_tab, 1)
            for n in range(2):
                nc.tensor.matmul(bank[n][0:16, :], tab[0:33, :], onehot[:, n * 512:(n + 1) * 512],
                                 start=True, stop=True).then_inc(s_bias, 1)
            pe.wait_ge(loaded("x"), 16)
            pe.wait_ge(loaded("cst"), 16)

            def x_transposes(k):
                for q in range(QT):
                    last = nc.tensor.transpose(XB[k][:, q * P:(q + 1) * P],
                                               xn[:, q, k * P:(k + 1) * P], ident)
                last.then_inc(s_xT, 1)
            for k in range(5):
                x_transposes(k)
            pe.wait_ge(s_bias_sb, 1)
            for k in range(5, 7):
                x_transposes(k)
            pe.wait_ge(s_silu, 2)
            for j in range(16):
                pe.wait_ge(loaded(f"ada1_{j // 8}"), 16)
                for k in range(KC):
                    last = nc.tensor.matmul(bank[7][:, j:j + 1], ada1[:, k, j * P:(j + 1) * P], siluc[:, k:k + 1],
                                            start=(k == 0), stop=(k == KC - 1))
            last.then_inc(s_ada, 1)
            pe.wait_ge(s_hT, 1)
            x_transposes(7)
            pe.wait_ge(loaded("w_in"), 16 * len(W_IN_MOVES))
            pe.wait_ge(s_hT, 4)
            pe.wait_ge(s_hTa, 4)
            for i, (tr, where, _dst) in enumerate(proj):
                if i >= 4:
                    pj_wait(pe, i - 4)
                b = bank[i % 4]
                for k in range(KC):
                    if not tr:
                        last = nc.tensor.matmul(b[:, 0:NATW], hT[:, k, where * P:(where + 1) * P],
                                                w_in[:, k, NAT:NAT + NATW], start=(k == 0), stop=(k == KC - 1))
                        continue
                    last = nc.tensor.matmul(b[:, :], w_in[:, k, where:where + P], hT[:, k, :], start=(k == 0), stop=(k == KC - 1))
                last.then_inc(s_proj, 1)
            pe.wait_ge(s_nat, 1)
            for q in range(QT):
                nc.tensor.transpose(bank[4][:, q * P:(q + 1) * P], nat[:, q, N_CKV:N_CKV + P], ident)
                last = nc.tensor.transpose(bank[5][:, q * P:(q + 1) * P], kin[:, q, :], ident)
            last.then_inc(s_ctr, 1)
            pe.wait_ge(s_cev, 1)
            for j in range(4):
                if j >= 2:
                    pe.wait_ge(s_kvev, 2 * j - 3 + 0)
                nc.tensor.matmul(bank[6][:, :] if j % 2 == 0 else bank[4][:, :],
                                 wukv[:, 0, 2 * j:2 * j + 2, :], ckvT, start=True, stop=True).then_inc(s_kv, 1)
                if j >= 1:
                    pe.wait_ge(s_kvev, 2 * j - 1 + 1)
                nc.tensor.matmul(bank[7][:, :], ckvT[:, j * P:(j + 1) * P],
                                 wukv[:, 1, :, :], start=True, stop=True).then_inc(s_kv, 1)
            pe.wait_ge(s_cev, 2)
            for n in range(24):
                q, h = n // 8 + 1, n % 8
                if n >= 4:
                    pe.wait_ge(s_relu, n - 3)
                else:
                    pj_wait(pe, NPJ - 4 + n)
                hs = slice((h % 2) * DH, (h % 2 + 1) * DH)
                nc.tensor.matmul(bank[n % 4][:, 0:(q + 1) * P], qiT[hs, h // 2, q * P:(q + 1) * P],
                                 kiT[hs, 0:(q + 1) * P], start=True, stop=True).then_inc(s_is, 1)
            pe.wait_ge(s_blk, 8)
            pe.wait_ge(loaded("w1"), 32)
            pe.wait_ge(s_cev, 2)
            for s in range(2):
                for f in range(2):
                    for l in range(LC):
                        last = nc.tensor.matmul(bank[5][:, (2 * s + f) * 62:(2 * s + f + 1) * 62],
                                                w1[:, s, l, f * P:(f + 1) * P],
                                                blk[:, s, l, :, :].rearrange("p g c -> p (g c)"),
                                                start=(l == 0), stop=(l == LC - 1))
            last.then_inc(s_hid, 1)
            pe.wait_ge(s_gel, 1)
            pe.wait_ge(s_kvev, 8)
            for g in range(NG):
                for f in range(2):
                    nc.tensor.matmul(bank[6][g * DH:(g + 1) * DH, 0:NCMP], w2[:, 0, f, :],
                                     gelu[:, 0, f, g * NCMP:(g + 1) * NCMP], start=(f == 0), stop=(f == 1))
                for f in range(2):
                    last = nc.tensor.matmul(bank[7][0:NCMP, g * DH:(g + 1) * DH], gelu[:, 1, f, g * NCMP:(g + 1) * NCMP],
                                            w2[:, 1, f, :], start=(f == 0), stop=(f == 1))
            last.then_inc(s_cmp, 1)
            pe.wait_ge(s_cmpev, 2)
            pe.wait_ge(s_relu, 24)

            for s in range(NU + 4):
                if s < 64 and s % 8 == 0:
                    h = s // 8
                    g, j = h // 4, h % 4
                    gs = slice(g * DH, (g + 1) * DH)
                    if h:
                        pe.wait_ge(s_cO, h)
                    for q in range(QT):
                        last = nc.tensor.matmul(bank[7][:, q * NCMP:(q + 1) * NCMP], qnT[gs, j, q * P:(q + 1) * P],
                                                kcmpT[gs, :], start=True, stop=True)
                    last.then_inc(s_cS, 1)
                if s < NU:
                    b, h, q = UNITS[s]
                    n = (q + 1) * P
                    if s >= 3:
                        pe.wait_ge(s_ttr, s - 2)
                    if b == DSA:
                        hs = slice((h % 2) * DH, (h % 2 + 1) * DH)
                        lhs, rhs = qdT[hs, h // 2, q * P:(q + 1) * P], kdT[hs, h // 2, 0:n]
                        if q:
                            pe.wait_ge(s_sel, q)
                            pe.wait_ge(s_idb, 1)
                            nc.tensor.matmul(bank[s % 3][:, 0:n], identb[:, :], selm[:, q - 1, 0:n], start=True, stop=False)
                    else:
                        gs = slice((h // 4) * DH, (h // 4 + 1) * DH)
                        lhs = qnT[gs, h % 4, q * P:(q + 1) * P]
                        rhs = (ksT if b == SLC else kwT)[gs, 0:n]
                    nc.tensor.matmul(bank[s % 3][:, 0:n], lhs, rhs, start=not (b == DSA and q), stop=True).then_inc(s_S, 1)
                if s < 64 and s % 8 == 4:
                    pe.wait_ge(s_cN, s // 8 + 1)
                    for q in range(QT):
                        last = nc.tensor.transpose(bank[7][0:NCMP, q * P:(q + 1) * P], Pc[:, q, :], ident)
                    last.then_inc(s_cT, 1)
                if s < 64 and s % 8 == 5:
                    pe.wait_ge(s_cTev, s // 8 + 1)
                    for q in range(QT):
                        last = nc.tensor.matmul(bank[7][:, q * DH:(q + 1) * DH], PcT[:, q * P:(q + 1) * P],
                                                vcmp[:, s // 32, :], start=True, stop=True)
                    last.then_inc(s_cPV, 1)
                if 0 <= s - 2 < NU:
                    u = s - 2
                    q = UNITS[u][2]
                    pe.wait_ge(s_exp, u + 1)
                    if u >= 2:
                        pe.wait_ge(s_Tev, u - 1)
                    for kb in range(q + 1):
                        last = nc.tensor.transpose(bank[3 + u % 2][:, kb * P:(kb + 1) * P], Sb[:, u % 4, kb * P:(kb + 1) * P], ident)
                    last.then_inc(s_T, 1)
                if 0 <= s - 3 < NU:
                    u = s - 3
                    b, h, q = UNITS[u]
                    pe.wait_ge(s_Tev, u + 1)
                    if u >= 2:
                        pe.wait_ge(s_oev, u - 1)
                    for kb in range(q + 1):
                        if b == DSA:
                            v = vd[:, kb, h * DH:(h + 1) * DH]
                        else:
                            c0 = (N_VS if b == SLC else N_VW) + (h // 4) * DH
                            v = nat[:, kb, c0:c0 + DH]
                        last = nc.tensor.matmul(bank[5 + u % 2][:, 0:DH], PTs[:, u % 4, kb * P:(kb + 1) * P], v,
                                                start=(kb == 0), stop=(kb == q))
                    last.then_inc(s_PV, 1)


            def ada_row(n):
                pe.wait_ge(loaded(f"ada{n // 2}"), 32)
                if n >= 2:
                    pe.wait_ge(s_rowev, n - 1)
                for k in range(KC):
                    last = nc.tensor.matmul(bank[7 if n % 2 == 0 else 0][:, :], siluc[:, k:k + 1].to_broadcast([P, P]), ada_half[n][:, k, :],
                                            start=(k == 0), stop=(k == KC - 1))
                last.then_inc(s_row, 1)
            ada_row(0)
            ada_row(1)
            pe.wait_ge(s_osc, 8)
            for k in range(KC):
                if k >= 4:
                    pe.wait_ge(s_mTev[k % 2], (k - 4) // 2 + 1)
                for q in range(QT):
                    last = nc.tensor.transpose(bank[1 + k % 4][:, q * P:(q + 1) * P], o[:, q, k * P:(k + 1) * P], ident)
                last.then_inc(s_mT, 1)
            for n in (2, 3, 4, 5):
                ada_row(n)
            pe.wait_ge(s_row, 6)
            pe.sem_inc(s_used, 4)
            pe.wait_ge(loaded("w_out"), 16)
            pe.wait_ge(s_mTev[0], 4)
            pe.wait_ge(s_mTev[1], 4)
            for q in range(QT):
                if q == 2:
                    ada_row(6)
                    ada_row(7)
                if q >= 2:
                    pe.wait_ge(s_yrd, q - 1)
                for k in range(KC):
                    for n in range(2):
                        last = nc.tensor.matmul(bank[1 + 2 * (q % 2) + n][:, :], mixT[:, k, q * P:(q + 1) * P], w_out[:, k, n * 512:(n + 1) * 512],
                                                start=(k == 0), stop=(k == KC - 1))
                last.then_inc(s_y, 1)
            pe.wait_ge(s_y, QT)
            pe.sem_inc(s_used, 4)
            pe.wait_ge(s_rowev, 8)
            pe.wait_ge(loaded("w_rt"), 32)
            for q in range(QT):
                pe.wait_ge(s_h2, q + 1)
                if q:
                    pe.wait_ge(s_rTev, 2 * q)
                for k in range(KC):
                    last = nc.tensor.transpose(bank[5 + k // 4][:, (k % 4) * P:(k % 4 + 1) * P], h2[:, q % 2, k * P:(k + 1) * P], ident)
                last.then_inc(s_rT, 1)
                pe.wait_ge(s_rTev, 2 * q + 2)
                if q:
                    pe.wait_ge(s_rlv, q)
                for k in range(KC):
                    last = nc.tensor.matmul(bank[7][:, 0:NE], h2T[:, k, :], w_rt[:, k, :], start=(k == 0), stop=(k == KC - 1))
                last.then_inc(s_rl, 1)
            pe.wait_ge(s_selb, QT)
            pe.wait_ge(s_trib, 1)
            for q in range(QT):
                for q2 in range(q + 1):
                    nc.tensor.matmul(bank[5][:, q * NE:(q + 1) * NE], trib[:, :] if q2 == q else cone[:, 0:P], selb[:, q2, :],
                                     start=(q2 == 0), stop=(q2 == q))
            for q in range(QT):
                last = nc.tensor.matmul(bank[6][:, 0:NE], cone[:, 0:P], selb[:, q, :], start=(q == 0), stop=(q == QT - 1))
            last.then_inc(s_pos, 1)
            pe.wait_ge(s_tables, 1)
            pe.sem_inc(s_used, 4)

            G, U, Y, TA = bank[0:2], bank[2:4], bank[4:6], bank[6:8]

            def slots(e):
                for q in range(QT):
                    last = nc.tensor.matmul(bank[7][:, 0:3], OH[:, q, :], TG[:, q, e, :], start=(q == 0), stop=(q == QT - 1))
                last.then_inc(s_rtm, 1)

            def rows_transposed(par):
                for k in range(KC):
                    last = nc.tensor.transpose(Y[k // 4][:, (k % 4) * P:(k % 4 + 1) * P], xg[par][:, k * P:(k + 1) * P], ident)
                last.then_inc(s_tx, 1)

            def bias(dst, m, par, half):
                nc.tensor.matmul(dst, onesb, bp[par][:, m * D + half * 512:m * D + (half + 1) * 512], start=True, stop=False)
            pe.wait_ge(s_oh, 1)
            slots(slice(0, 1))
            pe.wait_ge(s_g[0], 16)
            rows_transposed(0)
            n_rounds = pe.value_load(rounds_i[0:1, 0:1], min_val=1, max_val=QT)
            with pe.Fori(0, n_rounds) as rd:
                with pe.Fori(0, NE // 2) as ep:
                    for par in range(2):
                        i = rd * NE + ep * 2 + par
                        pair = rd * (NE // 2) + ep
                        h = hTe[par]
                        pe.wait_ge(s_gdr, i * 2)
                        pe.wait_ge(s_xe[0], i + 1)
                        pe.wait_ge(s_xe[1], i + 1)
                        pe.wait_ge(s_bp[par], pair * 16 + 16)
                        for half in range(2):
                            bias(G[half][:, :], 0, par, half)
                        for k in range(KC):
                            if k % 2 == 0:
                                pe.wait_ge(s_w[k // 2], i * 16 + 16)
                            for half in range(2):
                                last = nc.tensor.matmul(G[half][:, :], h[:, k, :], ring[:, k, half * 512:(half + 1) * 512],
                                                        start=False, stop=(k == KC - 1))
                            if k % 2:
                                last.then_inc(s_used, 1)
                        pe.wait_ge(s_oh, i + 2)
                        slots(ds(ep * 2 + (par + 1), 1))
                        pe.wait_ge(s_udr, i * 2)
                        for half in range(2):
                            bias(U[half][:, :], 1, par, half)
                            for k in range(KC):
                                if half == 0 and k % 2 == 0:
                                    pe.wait_ge(s_w[4 + k // 2], i * 16 + 16)
                                last = nc.tensor.matmul(U[half][:, :], h[:, k, :], ring[:, 8 + k, half * 512:(half + 1) * 512],
                                                        start=False, stop=(k == KC - 1))
                                if half == 1 and k % 2:
                                    last.then_inc(s_used, 1)
                            if half == 0:
                                last.then_inc(s_uh, 1)
                        pe.wait_ge(s_idx, i + 2)
                        for half in range(2):
                            pe.wait_ge(s_act, i * 2 + half + 1)
                            for k in range(4):
                                c = (4 * half + k) * P
                                last = nc.tensor.transpose(TA[half][:, k * P:(k + 1) * P], prod[:, c:c + P], ident)
                            last.then_inc(s_ta, 1)
                            if half == 0:
                                pe.wait_ge(s_g[1 - par], pair * 16 + 16 + 16 * par)
                                pe.wait_ge(s_yb, i * 2)
                                rows_transposed(1 - par)
                        pe.wait_ge(s_xe[0], i + 2)
                        pe.wait_ge(s_xe[1], i + 2)
                        for half in range(2):
                            bias(Y[half][:, :], 2, par, half)
                        for k in range(KC):
                            if k % 4 == 0:
                                pe.wait_ge(s_at, i * 2 + 1 + k // 4)
                            if k % 2 == 0:
                                pe.wait_ge(s_w[8 + k // 2], i * 16 + 16)
                            for half in range(2):
                                last = nc.tensor.matmul(Y[half][:, :], actT[:, k, :], ring[:, 16 + k, half * 512:(half + 1) * 512],
                                                        start=False, stop=(k == KC - 1))
                            if k % 2:
                                last.then_inc(s_used, 1)

        @block.scalar
        def _(act):
            act.wait_ge(loaded("c"), 16)
            nc.scalar.activation(siluc, cT, ACT.Sigmoid).then_inc(s_silu, 1)
            act.wait_ge(s_adaT, 2)
            for k in (1, 3, 5, 7):
                act.wait_ge(s_xT, k + 1)
                nc.scalar.activation(hT[:, k, :], XB[k][:, :], ACT.Identity, bias=adaT[:, k:k + 1],
                                     scale=adaT[:, 8 + k:9 + k]).then_inc(s_hTa, 1)
            for i in range(1, NPJ, 2):
                act.wait_ge(s_proj, i + 1)
                dst = proj[i][2]
                src = bank[i % 4][:, 0:dst.shape[-1]]
                sc = pj_scale(i)
                nc.scalar.activation(dst, src, ACT.Copy, scale=1.0 if sc is None else sc).then_inc(s_pev[1], 1)
                if i == 5:
                    pj_wait(act, 4)
                    pj_wait(act, 5)
                    nc.scalar.activation(gsig, nat[:, :, N_GATE:N_GATE + 24], ACT.Sigmoid).then_inc(s_gsig, 1)
                    act.wait_ge(s_kvar, 1)
                    nc.scalar.activation(rs4, rs4, ACT.Sqrt).then_inc(s_sqrt, 1)
                    nc.scalar.activation(rk4, rk4, ACT.Sqrt).then_inc(s_sqrt, 1)
            act.wait_ge(s_ctr, 1)
            act.wait_ge(loaded("small"), 16 * 13)
            nc.scalar.activation(ckvT, bank[4][:, :], ACT.Copy, scale=ckvg).then_inc(s_cev, 1)
            nc.scalar.activation(kiT, bank[5][:, :], ACT.Identity, scale=kig, bias=kib).then_inc(s_cev, 1)
            for j in range(4):
                act.wait_ge(s_kv, 2 * j + 1)
                nc.scalar.activation(kdT[:, j, :], (bank[6] if j % 2 == 0 else bank[4])[:, :], ACT.Copy).then_inc(s_kvev, 1)
                act.wait_ge(s_kv, 2 * j + 2)
                nc.scalar.activation(vd[:, j, :], bank[7][:, :], ACT.Copy).then_inc(s_kvev, 1)
            for n in range(24):
                q = n // 8 + 1
                act.wait_ge(s_is, n + 1)
                if n >= 4:
                    act.wait_ge(s_isc, n - 3)
                else:
                    act.wait_ge(s_blk, 8)
                nc.scalar.activation(Sb[:, n % 4, :][:, 0:(q + 1) * P], bank[n % 4][:, 0:(q + 1) * P], ACT.Relu).then_inc(s_relu, 1)
            act.wait_ge(s_ga, 1)
            nc.scalar.activation(gt1[:, :, :, :], gt1[:, :, :, :], ACT.Tanh, scale=math.sqrt(2 / math.pi)).then_inc(s_gt, 1)
            for s in range(NU + 4):
                if s < NU:
                    n = (UNITS[s][2] + 1) * P
                    act.wait_ge(s_ttr, s + 1)
                    nc.scalar.activation(Sb[:, s % 4, 0:n], Sb[:, s % 4, 0:n], ACT.Exp, scale=-1.0, bias=umin[:, s:s + 1],
                                         accum_out=usum[:, s:s + 1]).then_inc(s_exp, 1)
                if s < 64 and s % 8 == 1:
                    act.wait_ge(s_cSub, s // 8 + 1)
                    nc.scalar.activation(Pc, Pc, ACT.Exp, scale=-1.0).then_inc(s_cExp, 1)
                if s < 64 and s % 8 == 4:
                    act.wait_ge(s_cT, s // 8 + 1)
                    nc.scalar.activation(PcT, bank[7][0:NCMP, :], ACT.Copy).then_inc(s_cTev, 1)
                if 0 <= s - 2 < NU:
                    u = s - 2
                    n = (UNITS[u][2] + 1) * P
                    act.wait_ge(s_T, u + 1)
                    if u >= 4:
                        act.wait_ge(s_PV, u - 3)
                    nc.scalar.activation(PTs[:, u % 4, 0:n], bank[3 + u % 2][:, 0:n], ACT.Copy).then_inc(s_Tev, 1)

            act.wait_ge(s_oev, NU)
            act.wait_ge(s_cO, NH)
            for n in range(8):
                nc.scalar.activation(yt[:, 0, 0:512] if n % 2 else yt[:, 0, 512:1024], o[:, n // 2, (n % 2) * 512:(n % 2 + 1) * 512], ACT.Square,
                                     accum_out=ssq[:, n:n + 1]).then_inc(s_ssq, 1)
                act.wait_ge(s_ssq, n + 1)
            act.wait_ge(s_ms, 1)
            nc.scalar.activation(rr8, rr8, ACT.Sqrt).then_inc(s_rt, 1)
            for k in range(1, KC, 2):
                act.wait_ge(s_mT, k + 1)
                nc.scalar.activation(mixT[:, k, :], bank[1 + k % 4][:, :], ACT.Copy, scale=og[:, k:k + 1]).then_inc(s_mTev[1], 1)
            for q in range(QT):
                act.wait_ge(s_lv, q + 1)
                nc.scalar.activation(lnr[:, 0, q:q + 1], lnr[:, 0, q:q + 1], ACT.Sqrt).then_inc(s_lr, 1)
            for q in range(QT):
                act.wait_ge(s_rT, q + 1)
                if q:
                    act.wait_ge(s_rl, q)
                for n in range(2):
                    nc.scalar.activation(h2T[:, 4 * n:4 * n + 4, :], bank[5 + n][:, :].rearrange("p (k t) -> p k t", k=4), ACT.Copy).then_inc(s_rTev, 1)
            for q in range(QT):
                act.wait_ge(s_rnm, q + 1)
                nc.scalar.activation(ex4[:, q, :], lg[:, q, :], ACT.Exp, bias=rsm[:, 0, q:q + 1]).then_inc(s_rex, 1)

            def rowsT(par, half):
                nc.scalar.activation(hTe[par][:, 0:4, :], bank[4][:, :].rearrange("p (k t) -> p k t", k=4), ACT.Copy).then_inc(s_xe[1], 1)
            act.wait_ge(s_tx, 1)
            rowsT(0, 0)
            act.wait_ge(s_tables, 1)
            n_rounds = act.value_load(rounds_i[0:1, 0:1], min_val=1, max_val=QT)
            with act.Fori(0, n_rounds) as rd:
                with act.Fori(0, NE // 2) as ep:
                    for par in range(2):
                        i = rd * NE + ep * 2 + par
                        for half in range(2):
                            hs = slice(half * 512, (half + 1) * 512)
                            act.wait_ge(s_gdr, i * 2 + half + 1)
                            nc.scalar.activation(sgm[:, hs], gts[:, hs], ACT.Sigmoid, scale=1.702).then_inc(s_sig, 1)
                        act.wait_ge(s_ta, i * 2 + 1)
                        nc.scalar.activation(actT[:, 0:4, :], bank[6][:, :].rearrange("p (k t) -> p k t", k=4), ACT.Copy).then_inc(s_at, 1)
                        act.wait_ge(s_tx, i + 2)
                        rowsT(1 - par, 0)
                        act.wait_ge(s_ta, i * 2 + 2)
                        nc.scalar.activation(actT[:, 4:8, :], bank[7][:, :].rearrange("p (k t) -> p k t", k=4), ACT.Copy).then_inc(s_at, 1)
                        act.wait_ge(s_used, i * 12 + 24)
                        act.wait_ge(s_sc, i * 16)
                        for half in range(2):
                            nc.scalar.activation(yb[par][:, half * 512:(half + 1) * 512], bank[4 + half][:, :], ACT.Copy,
                                                 scale=slot_in[:, par, 1:2]).then_inc(s_yb, 1)
            for q in range(QT):
                act.wait_ge(s_fv, q + 1)
                nc.scalar.activation(lnr[:, 0, q:q + 1], lnr[:, 0, q:q + 1], ACT.Sqrt).then_inc(s_fr, 1)

        @block.vector
        def _(dve):
            own = [0]

            def link(ins):
                own[0] += 1
                ins.then_inc(chain_s["dve"], 1)
                dve.wait_ge(chain_s["dve"], own[0])

            dve.wait_ge(loaded("tab"), 16)
            nc.vector.memset(tab[32:33, :], 1.0).then_inc(s_tab, 1)
            dve.wait_ge(s_silu, 1)
            nc.vector.tensor_tensor(siluc, siluc, cT, ALU.mult).then_inc(s_silu, 1)
            for n in range(2):
                dve.wait_ge(s_bias, n + 1)
                last = nc.vector.tensor_copy(E_sb[:, n * 512:(n + 1) * 512], bank[n][0:16, :])
            last.then_inc(s_bias_sb, 1)
            dve.wait_ge(s_ada, 1)
            dve.wait_ge(loaded("bada"), 16)
            nc.vector.tensor_tensor(adaT[:, 0:8], bank[7][:, 0:8], badaT[:, 0:8], ALU.add).then_inc(s_adaT, 1)
            nc.vector.scalar_tensor_tensor(adaT[:, 8:16], bank[7][:, 8:16], 1.0, badaT[:, 8:16], ALU.add, ALU.add).then_inc(s_adaT, 1)
            dve.wait_ge(s_adaT, 2)
            for k in (0, 2, 4, 6):
                dve.wait_ge(s_xT, k + 1)
                nc.vector.tensor_scalar(hT[:, k, :], XB[k][:, :], adaT[:, 8 + k:9 + k], adaT[:, k:k + 1],
                                        ALU.mult, ALU.add).then_inc(s_hT, 1)
            for i in range(0, NPJ, 2):
                dve.wait_ge(s_proj, i + 1)
                dst = proj[i][2]
                src = bank[i % 4][:, 0:dst.shape[-1]]
                sc = pj_scale(i)
                if sc is None:
                    nc.vector.tensor_copy(dst, src).then_inc(s_pev[0], 1)
                else:
                    nc.vector.tensor_scalar(dst, src, sc, None, ALU.mult).then_inc(s_pev[0], 1)
                if i == 4:
                    pj_wait(dve, 3)
                    pj_wait(dve, 4)
                    pj_wait(dve, 5)
                    for q in range(QT):
                        c = nat[:, q, N_CKV:N_CKV + P]
                        nc.vector.tensor_tensor_reduce(out=score[:, q * P:(q + 1) * P], in0=c, in1=c, scale=1.0, scalar=0.0,
                                                       op0=ALU.mult, op1=ALU.add, accum_out=ss4[:, q:q + 1])
                        last = nc.vector.bn_stats(st[:, q, :], nat[:, q, N_KI:N_KI + DH])
                    link(last)
                    for q in range(QT):
                        last = nc.vector.bn_aggr(mv[:, q, :], st[:, q, :])
                    nc.vector.tensor_scalar(rs4, ss4, 1.0 / P, 1e-6, ALU.mult, ALU.add)
                    link(last)
                    nc.vector.tensor_scalar(rk4, mv[:, :, 1], 1e-5, None, ALU.add).then_inc(s_kvar, 1)
                    nc.vector.tensor_scalar(wis, nat[:, :, N_WI:N_WI + NH], 8 ** -0.5 * DH ** -0.5, None, ALU.mult)
                    dve.wait_ge(s_sqrt, 2)
                    nc.vector.reciprocal(rs4, rs4)
                    link(nc.vector.reciprocal(rk4, rk4))
                    for q in range(QT):
                        c = nat[:, q, N_CKV:N_CKV + P]
                        nc.vector.tensor_scalar(c, c, rs4[:, q:q + 1], None, ALU.mult)
                        for half in range(2):
                            last = nc.vector.tensor_scalar(kin[:, q, half * DH:(half + 1) * DH], nat[:, q, N_KI:N_KI + DH],
                                                           mv[:, q, 0:1], rk4[:, q:q + 1], ALU.subtract, ALU.mult)
                    last.then_inc(s_nat, 1)
            dve.wait_ge(s_gsig, 1)
            dve.wait_ge(s_idb, 1)
            for n in range(24):
                q, h = n // 8 + 1, n % 8
                w = (q + 1) * P
                dve.wait_ge(s_relu, n + 1)
                sc = sel_s[:, q - 1, 0:w]
                if h == 0:
                    last = nc.vector.tensor_scalar(sc, Sb[:, n % 4, :][:, 0:w], wis[:, q, h:h + 1], None, ALU.mult)
                else:
                    dve.wait_ge(s_isc, n)
                    last = nc.vector.scalar_tensor_tensor(sc, Sb[:, n % 4, :][:, 0:w], wis[:, q, h:h + 1], sc, ALU.mult, ALU.add)
                last.then_inc(s_isc, 1)
                if h == 7:
                    dve.wait_ge(s_isc, n + 1)
                    link(nc.vector.tensor_tensor(sel_s[:, q - 1, q * P:(q + 1) * P], sel_s[:, q - 1, q * P:(q + 1) * P],
                                                 cst[:, C_CAUS:C_CAUS + P], ALU.add))
            dve.wait_ge(s_hid, 1)
            hid = bank[5][:, 0:248]
            g2 = gelu[:, :, :, :].rearrange("p a b c -> p (a b c)")
            g1 = gt1[:, :, :, :].rearrange("p a b c -> p (a b c)")
            link(nc.vector.tensor_copy(g2, hid))
            link(nc.vector.tensor_tensor(g1, g2, g2, ALU.mult))
            link(nc.vector.tensor_scalar(g1, g1, 0.044715, 1.0, ALU.mult, ALU.add))
            nc.vector.tensor_tensor(g1, g1, g2, ALU.mult).then_inc(s_ga, 1)
            dve.wait_ge(s_gt, 1)
            link(nc.vector.tensor_scalar(g1, g1, 0.5, 0.5, ALU.mult, ALU.add))
            nc.vector.tensor_tensor(g2, g2, g1, ALU.mult).then_inc(s_gel, 1)
            dve.wait_ge(s_cmp, 1)
            nc.vector.tensor_copy(kcmpT[:, :], bank[6][:, 0:NCMP]).then_inc(s_cmpev, 1)
            nc.vector.tensor_copy(vcmp[:, :, :], bank[7][0:NCMP, 0:128].rearrange("p (g d) -> p g d", g=2)).then_inc(s_cmpev, 1)

            def topk_round(n):
                q, r = n // 16 + 1, n % 16
                w = (q + 1) * P
                sc = sel_s[:, q - 1, 0:w]
                link(nc.vector.max(max8, sc if r == 0 else work[:, 0:w]))
                if r < 15:
                    link(nc.vector.match_replace(work[:, 0:w], max8, sc if r == 0 else work[:, 0:w], -3e38))
                    return
                gt, eq = score[:, 0:w], work[:, 0:w]
                nc.vector.tensor_scalar(eq, sc, max8[:, 7:8], None, ALU.is_equal)
                link(nc.vector.tensor_scalar(gt, sc, max8[:, 7:8], 0.0, ALU.is_gt, ALU.add, accum_out=cnt))
                nc.vector.tensor_scalar(need, cnt, -1.0, float(TOPK_KEYS), ALU.mult, ALU.add)
                link(nc.vector.tensor_tensor_scan(sc, cone[:, 0:w], eq, 0.0, ALU.mult, ALU.add))
                link(nc.vector.scalar_tensor_tensor(sc, sc, need, eq, ALU.is_le, ALU.mult))
                link(nc.vector.tensor_tensor(sc, sc, gt, ALU.add))
                nc.vector.tensor_scalar(selm[:, q - 1, 0:w], sc, -BIG, BIG, ALU.mult, ALU.add).then_inc(s_sel, 1)

            for s in range(NU + 5):
                if s < NU:
                    b, h, q = UNITS[s]
                    n = (q + 1) * P
                    m = h + (8 if b == DSA else 0)
                    dve.wait_ge(loaded(f"master{m % 2}"), 16 * (m // 2 + 1))
                    dve.wait_ge(s_S, s + 1)
                    if s >= 4:
                        dve.wait_ge(s_T, s - 3)
                    y0 = T - 1 + q * P - (MW - T if b == DSA else 0)
                    biases = bass.AP(tensor=master[:, :, :].tensor, offset=(m % 2) * MW + y0,
                                     ap=[list(master[:, :, :].ap[0]), [-1, n]])
                    nc.vector.tensor_tensor_reduce(out=Sb[:, s % 4, 0:n], in0=bank[s % 3][:, 0:n],
                                                   in1=biases, scale=1.0, scalar=3e38,
                                                   op0=ALU.add, op1=ALU.min, accum_out=umin[:, s:s + 1]).then_inc(s_ttr, 1)
                if s < 64 and s % 8 == 0:
                    h = s // 8
                    dve.wait_ge(s_cS, h + 1)
                    if h:
                        dve.wait_ge(s_cT, h)
                    y0 = T - CMP_LEN
                    mc = bass.AP(tensor=master[:, :, :].tensor, offset=(h % 2) * MW + y0,
                                 ap=[list(master[:, :, :].ap[0]), [P, QT], [-CMP_STRIDE, NCMP]])
                    link(nc.vector.tensor_tensor(Pc, bank[7][:, 0:QT * NCMP].rearrange("p (q c) -> p q c", q=QT), mc, ALU.add))
                    link(nc.vector.tensor_reduce(cm4[:, 0, :], Pc, AX.X, ALU.min))
                    nc.vector.tensor_tensor(Pc, Pc, cm4[:, 0, :].unsqueeze(2).to_broadcast([P, QT, NCMP]),
                                            ALU.subtract).then_inc(s_cSub, 1)
                if s < 64 and s % 8 == 2:
                    h = s // 8
                    dve.wait_ge(s_cExp, h + 1)
                    link(nc.vector.tensor_tensor(Pc, Pc,
                                                 cst[:, C_CMASK:C_CMASK + QT * NCMP].rearrange("p (q c) -> p q c", q=QT), ALU.mult))
                    link(nc.vector.tensor_reduce(cm4[:, 1, :], Pc, AX.X, ALU.add))
                    link(nc.vector.scalar_tensor_tensor(cm4[:, 2, :], cm4[:, 1, :], 0.0, cm4[:, 1, :], ALU.is_equal, ALU.add))
                    link(nc.vector.reciprocal(cm4[:, 3, :], cm4[:, 2, :]))
                    link(nc.vector.tensor_tensor(cm4[:, 3, :], cm4[:, 3, :], gsig[:, :, 3 * h], ALU.mult))
                    nc.vector.tensor_tensor(Pc, Pc, cm4[:, 3, :].unsqueeze(2).to_broadcast([P, QT, NCMP]),
                                            ALU.mult).then_inc(s_cN, 1)
                if 0 <= s - 8 < 48:
                    topk_round(s - 8)
                if 0 <= s - 4 < NU:
                    u = s - 4
                    b, h, q = UNITS[u]
                    dve.wait_ge(s_PV, u + 1)
                    r = rsum[:, u:u + 1]
                    link(nc.vector.reciprocal(r, usum[:, u:u + 1]))
                    ps = bank[5 + u % 2][:, 0:DH]
                    if b == DSA:
                        dst = o[:, q, 512 + h * DH:512 + (h + 1) * DH]
                    else:
                        dst = o[:, q, h * DH:(h + 1) * DH]
                        link(nc.vector.tensor_tensor(r, r, gsig[:, q, 3 * h + 1 + b:3 * h + 2 + b], ALU.mult))
                    if b != WIN:
                        nc.vector.tensor_scalar(dst, ps, r, None, ALU.mult).then_inc(s_oev, 1)
                    else:
                        dve.wait_ge(s_oev, u - 3)
                        dve.wait_ge(s_cO, h + 1)
                        nc.vector.scalar_tensor_tensor(dst, ps, r, dst, ALU.mult, ALU.add).then_inc(s_oev, 1)
                if s < 64 and s % 8 == 7:
                    h = s // 8
                    dve.wait_ge(s_cPV, h + 1)
                    dve.wait_ge(s_oev, 8 * h + 4)
                    oo = o[:, :, h * DH:(h + 1) * DH]
                    nc.vector.tensor_tensor(oo, oo, bank[7][:, 0:QT * DH].rearrange("p (q d) -> p q d", q=QT), ALU.add).then_inc(s_cO, 1)


            def ada_row(n):
                r = (0, 0, 1, 1, 2, 2, 5, 5)[n]
                dst = rows[r][:, (n % 2) * 512:(n % 2 + 1) * 512]
                dve.wait_ge(loaded(f"rows{r // 4}"), 64)
                dve.wait_ge(s_row, n + 1)
                nc.vector.scalar_tensor_tensor(dst, bank[7 if n % 2 == 0 else 0][:, :], 0.0 if r == 2 else 1.0, dst,
                                               ALU.add, ALU.add).then_inc(s_rowev, 1)
            dve.wait_ge(s_ssq, 8)
            nc.vector.tensor_scalar(rr8, ssq, 1.0 / 512, 1e-6, ALU.mult, ALU.add).then_inc(s_ms, 1)
            dve.wait_ge(s_rt, 1)
            link(nc.vector.reciprocal(rr8, rr8))
            for n in range(8):
                oo = o[:, n // 2, (n % 2) * 512:(n % 2 + 1) * 512]
                nc.vector.tensor_scalar(oo, oo, rr8[:, n:n + 1], None, ALU.mult).then_inc(s_osc, 1)
            ada_row(0)
            ada_row(1)
            for k in range(0, KC, 2):
                dve.wait_ge(s_mT, k + 1)
                nc.vector.tensor_scalar(mixT[:, k, :], bank[1 + k % 4][:, :], og[:, k:k + 1], None, ALU.mult).then_inc(s_mTev[0], 1)
            for n in (2, 3, 4, 5):
                ada_row(n)

            def statistics(src, q):
                for half in range(2):
                    last = nc.vector.bn_stats(lnst[:, q, half * 6:(half + 1) * 6], src[:, half * 512:(half + 1) * 512])
                link(last)
                link(nc.vector.bn_aggr(lnmv[:, q, :], lnst[:, q, :].rearrange("p (a b) -> p a b", a=2)))
                return nc.vector.tensor_scalar(lnr[:, 0, q:q + 1], lnmv[:, q, 1:2], 1e-5, None, ALU.add)
            dve.wait_ge(loaded("x_again"), 16)
            dve.wait_ge(s_rowev, 2)
            dve.wait_ge(s_ab, 1)
            for q in range(QT):
                dve.wait_ge(s_y, q + 1)
                t = yt[:, q % 2, :]
                if q >= 2:
                    dve.wait_ge(s_x1, q - 1)
                    dve.wait_ge(s_h2, q - 1)
                for half in range(2):
                    hs = slice(half * 512, (half + 1) * 512)
                    last = nc.vector.tensor_tensor(t[:, hs], bank[1 + 2 * (q % 2) + half][:, :], g1r[:, hs], ALU.mult)
                last.then_inc(s_yrd, 1)
                dve.wait_ge(s_yrd, q + 1)
                link(nc.vector.scalar_tensor_tensor(t, x1[:, q, :], ALPHA, t, ALU.mult, ALU.add))
                statistics(t, q).then_inc(s_lv, 1)
                dve.wait_ge(s_lr, q + 1)
                link(nc.vector.reciprocal(lnr[:, 1, q:q + 1], lnr[:, 0, q:q + 1]))
                nc.vector.tensor_scalar(t, t, lnmv[:, q, 0:1], lnr[:, 1, q:q + 1], ALU.subtract, ALU.mult).then_inc(s_xh, 1)
                dve.wait_ge(s_xh, q + 1)
                if q >= 2:
                    dve.wait_ge(s_h2st[q % 2], 16)
                    dve.wait_ge(s_rT, q - 1)
                link(nc.vector.tensor_tensor(h2[:, q % 2, :], t, sc2r, ALU.mult))
                nc.vector.tensor_tensor(h2[:, q % 2, :], h2[:, q % 2, :], sh2r, ALU.add).then_inc(s_h2, 1)
                if q == 1:
                    ada_row(6)
                    ada_row(7)
            dve.wait_ge(loaded("w_rt"), 32)
            for q in range(QT):
                dve.wait_ge(s_rl, q + 1)
                nc.vector.tensor_tensor(lg[:, q, :], bank[7][:, 0:NE], b_rt, ALU.add).then_inc(s_rlv, 1)
                dve.wait_ge(s_rlv, q + 1)
                link(nc.vector.max(m8[:, q, :], lg[:, q, :]))
                nc.vector.tensor_scalar(rsm[:, 0, q:q + 1], m8[:, q, 0:1], -1.0, None, ALU.mult).then_inc(s_rnm, 1)
                nc.vector.tensor_scalar(eq4[:, q, :], lg[:, q, :], m8[:, q, 3:4], None, ALU.is_equal)
                link(nc.vector.tensor_scalar(sel[:, q, :], lg[:, q, :], m8[:, q, 3:4], 0.0, ALU.is_gt, ALU.add, accum_out=rsm[:, 1, q:q + 1]))
                nc.vector.tensor_scalar(rsm[:, 2, q:q + 1], rsm[:, 1, q:q + 1], -1.0, float(TOPK_EXP), ALU.mult, ALU.add)
                link(nc.vector.tensor_tensor_scan(cum4[:, q, :], cone[:, 0:NE], eq4[:, q, :], 0.0, ALU.mult, ALU.add))
                link(nc.vector.scalar_tensor_tensor(cum4[:, q, :], cum4[:, q, :], rsm[:, 2, q:q + 1], eq4[:, q, :], ALU.is_le, ALU.mult))
                link(nc.vector.tensor_tensor(sel[:, q, :], sel[:, q, :], cum4[:, q, :], ALU.add))
                nc.vector.tensor_copy(selb[:, q, :], sel[:, q, :]).then_inc(s_selb, 1)
            dve.wait_ge(loaded("cst"), 16)
            for q in range(QT):
                dve.wait_ge(s_rex, q + 1)
                link(nc.vector.tensor_tensor(ex4[:, q, :], ex4[:, q, :], sel[:, q, :], ALU.mult))
            link(nc.vector.tensor_reduce(rsm[:, 3, :], ex4, AX.X, ALU.add))
            link(nc.vector.reciprocal(rsm[:, 4, :], rsm[:, 3, :]))
            nc.vector.memset(TG, 1.0)
            link(nc.vector.memset(posr, -1.0))
            for q in range(QT):
                nc.vector.tensor_scalar(TG[:, q, 0:NE, 1], ex4[:, q, :], rsm[:, 4, q:q + 1], None, ALU.mult)
                last = nc.vector.tensor_scalar(TG[:, q, :, 0], TG[:, q, :, 2], cst[:, C_TV + q:C_TV + q + 1], None, ALU.mult)
            link(last)
            link(nc.vector.tensor_copy(TG[:, :, NE, :], TG[:, :, 0, :]))
            dve.wait_ge(s_pos, 1)
            link(nc.vector.scalar_tensor_tensor(cum4, bank[5][:, 0:128].rearrange("p (q e) -> p q e", q=QT), 1e4, sel, ALU.add, ALU.mult))
            for rd in range(QT):
                last = nc.vector.tensor_scalar(posr[:, :, rd * NE:(rd + 1) * NE], cum4, -1e4 - P * rd, None, ALU.add)
            link(last)
            link(nc.vector.tensor_reduce(most[:, 0:1], bank[6][:, 0:NE], AX.X, ALU.max))
            link(nc.vector.tensor_scalar(most[:, 1:2], most[:, 0:1], float(P), 1.0, ALU.is_gt, ALU.add))
            link(nc.vector.scalar_tensor_tensor(most[:, 1:2], most[:, 0:1], float(2 * P), most[:, 1:2], ALU.is_gt, ALU.add))
            link(nc.vector.scalar_tensor_tensor(most[:, 1:2], most[:, 0:1], float(3 * P), most[:, 1:2], ALU.is_gt, ALU.add))
            nc.vector.tensor_copy(rounds_i, most[:, 1:2]).then_inc(s_tables, 1)
            dve.wait_ge(s_tables, 1)

            own_e = sem_e

            def one_hot(col):
                for q in range(QT):
                    last = nc.vector.tensor_scalar(OH[:, q, :], cst[:, C_IOTA:C_IOTA + P], posr[:, q, col], None, ALU.is_equal)
                last.then_inc(s_oh, 1)

            def slot_indices(par, base):
                nc.vector.tensor_copy(slot_in[:, par, 0:3], bank[7][:, 0:3]).then_inc(own_e, 1)
                dve.wait_ge(own_e, base + 1)
                nc.vector.tensor_copy(idx_g[:, par:par + 1], slot_in[:, par, 0:1])
                nc.vector.scalar_tensor_tensor(slot_t[:, par:par + 1], slot_in[:, par, 2:3], cst[:, C_NDUM:C_NDUM + 1], slot_in[:, par, 0:1],
                                               ALU.mult, ALU.add).then_inc(own_e, 1)
                dve.wait_ge(own_e, base + 2)
                nc.vector.tensor_scalar(idx_s[:, par:par + 1], slot_t[:, par:par + 1], cst[:, C_DUM:C_DUM + 1], None, ALU.add).then_inc(s_idx, 1)

            def rowsT(par):
                nc.vector.tensor_copy(hTe[par][:, 4:8, :], bank[5][:, :].rearrange("p (k t) -> p k t", k=4)).then_inc(s_xe[0], 1)
            one_hot(slice(0, 1))
            dve.wait_ge(s_rtm, 1)
            slot_indices(0, 0)
            dve.wait_ge(s_tx, 1)
            rowsT(0)
            n_rounds = dve.value_load(rounds_i[0:1, 0:1], min_val=1, max_val=QT)
            OWN = 3
            with dve.Fori(0, n_rounds) as rd:
                with dve.Fori(0, NE // 2) as ep:
                    for par in range(2):
                        i = rd * NE + ep * 2 + par
                        dve.wait_ge(s_rtm, i + 1)
                        one_hot(ds(i + 1, 1))
                        dve.wait_ge(s_used, i * 12 + 16)
                        for half in range(2):
                            hs = slice(half * 512, (half + 1) * 512)
                            nc.vector.tensor_scalar(gts[:, hs], bank[half][:, :], 7.0, None, ALU.min).then_inc(s_gdr, 1)
                        dve.wait_ge(s_rtm, i + 2)
                        dve.wait_ge(s_sc, i * 16)
                        slot_indices(1 - par, i * OWN + 2)
                        for half in range(2):
                            hs = slice(half * 512, (half + 1) * 512)
                            dve.wait_ge(s_sig, i * 2 + half + 1)
                            last = nc.vector.tensor_tensor(gts[:, hs], gts[:, hs], sgm[:, hs], ALU.mult)
                        last.then_inc(own_e, 1)
                        dve.wait_ge(own_e, i * OWN + 5)
                        for half in range(2):
                            hs = slice(half * 512, (half + 1) * 512)
                            if half == 0:
                                dve.wait_ge(s_uh, i + 1)
                            else:
                                dve.wait_ge(s_used, i * 12 + 20)
                            nc.vector.tensor_scalar(ucl[:, hs], bank[2 + half][:, :], 7.0, -7.0, ALU.min, ALU.max).then_inc(s_udr, 1)
                            dve.wait_ge(s_udr, i * 2 + half + 1)
                            nc.vector.scalar_tensor_tensor(prod[:, hs], ucl[:, hs], 1.0, gts[:, hs], ALU.add, ALU.mult).then_inc(s_act, 1)
                        dve.wait_ge(s_act, i * 2 + 2)
                        dve.wait_ge(s_tx, i + 2)
                        rowsT(1 - par)

            dve.wait_ge(s_al, 16)
            dve.wait_ge(loaded("rows1"), 64)
            for q in range(QT):
                t = ft[:, q, :]
                link(nc.vector.tensor_tensor(t, acc[:, q, :], g2r, ALU.mult))
                link(nc.vector.tensor_tensor(t, t, x1[:, q, :], ALU.add))
                statistics(t, q).then_inc(s_fv, 1)
                dve.wait_ge(s_fr, q + 1)
                link(nc.vector.reciprocal(lnr[:, 1, q:q + 1], lnr[:, 0, q:q + 1]))
                nc.vector.tensor_scalar(t, t, lnmv[:, q, 0:1], lnr[:, 1, q:q + 1], ALU.subtract, ALU.mult).then_inc(s_fh, 1)
                if q % 2:
                    dve.wait_ge(s_fh, q + 1)
                    link(nc.vector.tensor_tensor(t, t, ln2g, ALU.mult))
                    dve.wait_ge(s_fo, q)
                    nc.vector.tensor_tensor(t, t, ln2b, ALU.add).then_inc(s_fo, 1)
        blocks.close()


def constants():
    col = np.arange(EW)
    dist = col - (T - 1)
    d = np.maximum(dist, 1).astype(np.float32)
    large = 16 + (np.log(d / 16) / math.log(128 / 16) * 16).astype(np.int32)
    bucket = np.where(dist < 16, np.maximum(dist, 0), np.minimum(large, N_BUCKETS - 1))
    onehot = np.zeros((N_BUCKETS + 1, EW), np.float32)
    onehot[bucket[dist >= 0], col[dist >= 0]] = -1
    onehot[N_BUCKETS, dist < 0] = BIG
    cst = np.zeros((P, C_W), np.float32)
    p, n = np.arange(P)[:, None], np.arange(P)[None, :]
    cst[:, C_ID:C_ID + P] = p == n
    cst[:, C_TRI:C_TRI + P] = p < n
    cst[:, C_IOTA:C_IOTA + P] = n
    tok = np.arange(QT)[None, :, None] * P + p[:, :, None]
    key = np.arange(NCMP)[None, None, :] * CMP_STRIDE + CMP_LEN - 1
    cst[:, C_CMASK:C_CMASK + QT * NCMP] = (tok >= key).reshape(P, -1)
    cst[:, C_CAUS:C_CAUS + P] = np.where(n <= p, 0, -BIG)
    cst[:, C_TV:C_TV + QT] = np.arange(QT)[None, :] * P + p
    cst[:, C_DUM] = T + np.arange(P)
    cst[:, C_NDUM] = -(T + np.arange(P))
    return {"k_cst": cst, "k_onehot": onehot}


def kernel(**inputs):
    import concourse.bacc as bacc
    from concourse.bass_utils import run_bass_kernel_spmd

    nc = bacc.Bacc("TRN2", target_bir_lowering=False, num_devices=1)
    arrays, aps = {}, {}
    for name, value in list(inputs.items()) + list(constants().items()):
        value = np.ascontiguousarray(value)
        arrays[f"in_{name}"] = value
        aps[name] = nc.dram_tensor(f"in_{name}", value.shape, mybir.dt.from_np(value.dtype), kind="ExternalInput").ap()
    out = nc.dram_tensor("out", (1, T, D), mybir.dt.float32, kind="ExternalOutput").ap()
    build_layer(nc, aps, out)
    r = run_bass_kernel_spmd(nc, [arrays], core_ids=[0])
    return r.results[0]["out"]
```

```python
import math
from contextlib import ExitStack

import concourse.bass as bass
import numpy as np
from concourse import mybir

T = 512
D = 1024
P = 128
QT = T // P
KC = D // P
DH = 64
NH = 8
NG = 2
CMP_LEN, CMP_STRIDE = 32, 16
NCMP = (T - CMP_LEN) // CMP_STRIDE + 1
LC = CMP_LEN * DH // P
FH = 256
TOPK_KEYS = min(256, T // 4)
NE = 32
TOPK_EXP = 4
BIG = 1e30
ALPHA = 2 ** 0.25
N_BUCKETS = 32
EW = 1024
MW = 896
IN_COLS = 2528

W_IN_MOVES = [(512, 512, 384), (1024, 896, 128), (896, 2048, 128), (1152, 2176, 152),
              (1816, 2328, 128), (2456, 2456, 72), (1944, 1536, 512)]
W_IN_MOVES += [(256 * g + 64 * j, 128 * j + 64 * g, 64) for j in range(4) for g in range(2)]
W_IN_MOVES += [(1304, 1024, 512)]
QN, KCC, VCC, KSC, KWC, QD, QI, NAT = 0, 512, 640, 768, 896, 1024, 1536, 2048
NATW = 480
N_VS, N_VW, N_GATE, N_CKV, N_KI, N_WI = 0, 128, 256, 280, 408, 472

SLC, WIN, DSA = 0, 1, 2
UNITS = [(b, h, q) for h in range(NH) for b in (SLC, WIN) for q in range(QT)]
UNITS += [(DSA, h, q) for h in range(NH) for q in range(QT)]
NU = len(UNITS)

SL = 256
NR = T // SL
WIDTHS = tuple(range(P, SL + 1, 16))
SC = 4
NSLOT = 3 * KC // SC
NOWHERE = 4096

C_ID, C_TRI, C_IOTA, C_CMASK, C_CAUS, C_TV, C_W = 0, 128, 256, 384, 508, 636, 640


def build_layer(nc, a, out):
    f32, bf16, i32, u32 = mybir.dt.float32, mybir.dt.bfloat16, mybir.dt.int32, mybir.dt.uint32
    ALU, ACT, AX = mybir.AluOpType, mybir.ActivationFunctionType, mybir.AxisListType
    ds = bass.ds
    ctx = ExitStack()
    with ctx:
        def sb(name, shape, dt=f32):
            return ctx.enter_context(nc.sbuf_tensor(name, shape, dt))

        def sem(name):
            return ctx.enter_context(nc.semaphore(name))

        ring = sb("ring", [P, 24, D])
        att = sb("att", [P, 16384])
        hT = sb("hT", [P, KC, T])
        pa = sb("pa", [P, 4096])
        ringf = ring[:, :, :].rearrange("p a b -> p (a b)")
        hTf = hT[:, :, :].rearrange("p a b -> p (a b)")
        w_in = ringf[:, 0:KC * IN_COLS].rearrange("p (k n) -> p k n", k=KC)
        w1 = ringf[:, 0:8192].rearrange("p (s l f) -> p s l f", s=2, l=LC)
        ada1 = att[:, :].rearrange("p (k n) -> p k n", k=KC)

        def part(first, *shape):
            n = 1
            for s in shape:
                n *= s
            v = att[:, first:first + n]
            if len(shape) == 2:
                v = v.rearrange("p (a b) -> p a b", a=shape[0])
            return v
        qnT = part(0, 4, T)
        kcT, vcT, ksT, kwT = (part(2048 + 512 * n, T) for n in range(4))
        qdT = part(4096, 4, T)
        qiT = part(6144, 4, T)
        nat = part(8192, QT, NATW)
        kdT = part(10112, 4, T)
        vd = part(12160, QT, T)
        ckvT = part(14208, T)
        kiT = part(14720, T)
        score = part(15232, T)
        work = part(15744, T)
        ada_row1 = hTf[0:1, 0:2 * D]
        o = hTf.rearrange("p (q n) -> p q n", q=QT)
        xn = pa[:, :].rearrange("p (q n) -> p q n", q=QT)
        Sb = pa[:, 0:2048].rearrange("p (u n) -> p u n", u=4)
        PTs = pa[:, 2048:4096].rearrange("p (u n) -> p u n", u=4)
        X = pa[:, 0:2048].rearrange("p (s g t) -> p s g t", s=2, g=NG)
        blk = pa[:, 2048:2048 + 2 * LC * NG * NCMP].rearrange("p (s l g c) -> p s l g c", s=2, l=LC, g=NG)
        mixT = pa[:, :].rearrange("p (k t) -> p k t", k=KC)

        cst = sb("cst", [P, C_W])
        ident = cst[:, C_ID:C_ID + P]
        identb = sb("identb", [P, P], bf16)
        master = sb("master", [P, 2, MW])
        onehot = master[0:N_BUCKETS + 1, 0:2, :].rearrange("p a b -> p (a b)")[:, 0:EW]
        small = sb("small", [P, 600])
        cT, siluc = small[:, 0:8], small[:, 8:16]
        badaT, adaT = small[:, 16:32], small[:, 32:48]
        ckvg, kig, kib = small[:, 48:49], small[:, 49:50], small[:, 50:51]
        og = small[:, 52:60]
        tab = small[:, 60:76]
        pos2 = small[:, 76:108].rearrange("p (s l) -> p s l", s=2)
        gsig = small[:, 108:204].rearrange("p (q n) -> p q n", q=QT)
        wis = small[:, 204:236].rearrange("p (q n) -> p q n", q=QT)
        st = small[:, 236:260].rearrange("p (q n) -> p q n", q=QT)
        mv = small[:, 260:268].rearrange("p (q n) -> p q n", q=QT)
        ss4, rs4, rk4 = small[:, 268:272], small[:, 272:276], small[:, 276:280]
        usum, umin = small[:, 280:376], small[:, 376:472]
        rsum = small[:, 472:568]
        max8 = small[:, 568:576]
        cnt, need = small[:, 576:577], small[:, 577:578]
        ssq, rr8 = small[:, 580:588], small[:, 588:596]
        kin = work.rearrange("p (q n) -> p q n", q=QT)
        w2 = sb("w2", [P, 2, 2, DH])
        wukv = ringf[:, 20480:21504].rearrange("p (s h d) -> p s h d", s=2, h=NH)
        sel_s = ringf[:, 21504:23040].rearrange("p (q t) -> p q t", q=3)
        E_sb = ringf[0:16, 21504:21504 + EW]
        selm = ringf[:, 23040:23808].bitcast(bf16).rearrange("p (q t) -> p q t", q=3)
        PcT = ringf[0:NCMP, 23808:24320]
        cone = ringf[:, 24320:24576].bitcast(bf16)
        gelu = sb("gelu", [P, 2, 2, 2 * NCMP])
        gt1 = sb("gt1", [P, 2, 2, 2 * NCMP])
        kcmpT = sb("kcmpT", [P, NCMP])
        vcmp = sb("vcmp", [NCMP, NG, DH])
        Pc = part(16256, QT, NCMP)
        cm4 = sb("cm4", [P, 4, QT])

        bank = [ctx.enter_context(nc.psum_tensor(f"bank{n}", [P, 512], f32)) for n in range(8)]

        XB = [bank[n] for n in (2, 3, 4, 5, 6, 0, 1, 2)]
        e_d = nc.dram_tensor("bias_by_distance", (16, EW), f32).ap()

        w_out = ringf[:, 8192:16384].rearrange("p (k n) -> p k n", k=KC)
        ada_ring = [ringf[:, n * 4096:(n + 1) * 4096].rearrange("p (k n) -> p k n", k=KC) for n in range(2)]
        ada_att = [att[:, 8192 + n * 4096:8192 + (n + 1) * 4096].rearrange("p (k n) -> p k n", k=KC) for n in range(2)]
        ada_half = ada_ring + ada_att + ada_ring + ada_att
        rows = [att[:, n * D:(n + 1) * D] for n in range(8)]
        g1r, sc2r, sh2r, ln1g, ln1b, g2r, ln2g, ln2b = rows
        b_f32 = att[0:NE, 8192:8192 + 3 * D].rearrange("e (m n) -> e m n", m=3)
        biasT = att[:, 11264:11264 + 3 * KC * NE].rearrange("p (m k e) -> p m k e", m=3, k=KC)
        x1 = o
        yt = ringf[:, 16384:18432].rearrange("p (u n) -> p u n", u=2)
        h2 = ringf[:, 18432:20480].rearrange("p (u n) -> p u n", u=2)
        h2T = ringf[:, 20480:21504].rearrange("p (k t) -> p k t", k=KC)
        zero = ringf[:, 21504:22528]
        w_rt = ringf[:, 22528:22784].rearrange("p (k e) -> p k e", k=KC)
        b_rt = ringf[:, 22784:22816]
        ms = master[:, :, :].rearrange("p a b -> p (a b)")
        TG = ms[:, 0:408].bitcast(bf16).rearrange("p (q e n) -> p q e n", q=QT, n=6)
        posr = ms[:, 408:672].rearrange("p (q n) -> p q n", q=QT)
        held, full, fulls = ms[:, 672:737], ms[:, 737:802], ms[:, 802:867]
        held_i, fulls_i = ms[:, 867:932].bitcast(i32), ms[:, 932:997].bitcast(i32)
        lg, sel, eq4, cum4, ex4 = (ms[:, 928 + 128 * n:1056 + 128 * n].rearrange("p (q e) -> p q e", q=QT) for n in range(5))
        selb = ms[:, 1568:1632].bitcast(bf16).rearrange("p (q e) -> p q e", q=QT)
        m8 = ms[:, 1632:1664].rearrange("p (q n) -> p q n", q=QT)
        rsm = ms[:, 1664:1696].rearrange("p (n q) -> p n q", q=QT)
        rounds_i = ms[:, 1696:1697].bitcast(i32)
        most = ms[:, 1697:1700]
        slot_t = ms[:, 1712:1714]
        idx_g = ms[:, 1778:1780].bitcast(u32)
        idx_s = ms[:, 1780:1782].bitcast(u32)
        wgt, wnext = ms[:, 1782:1784], ms[:, 1784:1786]
        lnst = ms[:, 1714:1762].rearrange("p (q n) -> p q n", q=QT)
        lnmv = ms[:, 1762:1770].rearrange("p (q n) -> p q n", q=QT)
        lnr = ms[:, 1770:1778].rearrange("p (n q) -> p n q", q=QT)
        trib = identb

        hTe = att[:, 0:2048].rearrange("p (k t) -> p k t", k=KC)
        prod = att[:, 2048:4096].rearrange("p (k t) -> p k t", k=KC)
        gcl = att[:, 4096:4608].rearrange("p (u t) -> p u t", u=2)
        sgm = att[:, 4608:5120].rearrange("p (u t) -> p u t", u=2)
        xg = att[:, 8192:10240].rearrange("p (u n) -> p u n", u=2)
        OH = att[:, 10240:10752].bitcast(bf16).rearrange("p (q n) -> p q n", q=QT)
        yT = att[:, 12032:14080].rearrange("p (k t) -> p k t", k=KC)
        yb = att[:, 14080:16128].rearrange("p (u n) -> p u n", u=2)
        iota = pa[:, 0:SL]
        ucl = pa[:, 256:768].rearrange("p (u t) -> p u t", u=2)
        bcur = pa[:, 768:792].rearrange("p (m k) -> p m k", m=3)
        acc = ringf[:, 0:4096].rearrange("p (q n) -> p q n", q=QT)
        ft = ringf[:, 4096:8192].rearrange("p (q n) -> p q n", q=QT)

        h2_d = nc.dram_tensor("moe_input", (T, D), f32).ap()
        acc_d = nc.dram_tensor("moe_output", (T, D), f32).ap()

        loads = {}

        def loaded(name):
            if name not in loads:
                loads[name] = sem("ld_" + name)
            return loads[name]
        chain_s = {k: sem("own_" + k) for k in ("dve", "act", "pool")}
        s_bias = sem("bias_table_ready")
        s_bias_sb = sem("bias_table_in_sbuf")
        s_silu = sem("silu_ready")
        s_xT = sem("xT_ready")
        s_ada = sem("ada_ready")
        s_arow, s_arowev = sem("ada_part1_row_done"), sem("ada_part1_row_in_sbuf")
        s_adaT = sem("ada_columns_ready")
        s_hT = sem("hT_ready")
        s_proj = sem("proj_done")
        s_pev = [sem("proj_evac_dve"), sem("proj_evac_act")]
        s_nat = sem("norms_ready")
        s_sqrt = sem("sqrt_done")
        s_kvar = sem("variances_ready")
        s_ctr = sem("ckv_ki_transposed")
        s_cev = sem("ckv_ki_in_sbuf")
        s_kv = sem("dsa_kv_done")
        s_kvev = sem("dsa_kv_in_sbuf")
        s_X = sem("shifted_ready")
        s_blk = sem("blocks_ready")
        s_hid = sem("hidden_ready")
        s_gel = sem("gelu_ready")
        s_ga = sem("gelu_arg_ready")
        s_gt = sem("gelu_tanh_ready")
        s_cmp = sem("compressed_ready")
        s_cmpev = sem("compressed_in_sbuf")
        s_is = sem("index_scores_done")
        s_relu = sem("relu_ready")
        s_isc = sem("index_score_used")
        s_S = sem("logits_done")
        s_ttr = sem("biased_ready")
        s_exp = sem("exp_ready")
        s_T = sem("probs_transposed")
        s_Tev = sem("probsT_in_sbuf")
        s_PV = sem("pv_done")
        s_oev = sem("o_updated")
        s_sel = sem("selection_ready")
        s_cS, s_cSub, s_cExp, s_cN = sem("cmp_logits"), sem("cmp_shifted"), sem("cmp_exp"), sem("cmp_probs")
        s_cT, s_cTev, s_cPV, s_cO = sem("cmp_T"), sem("cmp_T_in_sbuf"), sem("cmp_pv"), sem("cmp_added")
        s_hTa, s_gsig, s_tab, s_idb = sem("hT_ready_act"), sem("gates_ready"), sem("table_row_ready"), sem("ident_bf16_ready")
        sem_e = sem("own_dve_experts")

        s_row, s_rowev = sem("ada_row_done"), sem("ada_row_in_sbuf")
        s_ssq, s_ms, s_rt, s_osc = sem("squares_summed"), sem("mean_square"), sem("root_ready"), sem("o_scaled")
        s_mT, s_mTev = sem("mix_transposed"), [sem("mixT_dve"), sem("mixT_act")]
        s_y, s_yrd = sem("w_out_done"), sem("y_used")
        s_lv, s_lr, s_xh, s_h2, s_h2st = sem("ln_var"), sem("ln_root"), sem("xhat_ready"), sem("h2_ready"), [sem(f"h2_stored{n}") for n in range(2)]
        s_ab, s_x1 = sem("ln_rows_ready"), sem("x1_ready")
        s_rT, s_rTev, s_rl, s_rlv, s_rex, s_rnm = sem("h2_transposed"), sem("h2T_in_sbuf"), sem("router_logits"), sem("router_logits_used"), sem("router_exp"), sem("router_max")
        s_selb, s_trib, s_pos, s_tables = sem("selected_ready"), sem("tri_ready"), sem("positions_done"), sem("tables_ready")
        s_zero, s_zst = sem("zero_ready"), sem("moe_output_zeroed")
        s_bT, s_bTev, s_bready = sem("biases_transposed"), sem("biasT_in_sbuf"), sem("biases_ready")
        s_mm = sem("products_done")
        s_w = [sem(f"slot{n}_loaded") for n in range(NSLOT)]
        s_oh, s_rtm, s_idx = sem("one_hot_ready"), sem("slots_done"), sem("slot_indices_ready")
        s_g, s_gd = [sem(f"gathered_tile{n}") for n in range(2)], sem("gathered")
        s_tx, s_xe = sem("rows_transposed"), [sem("rowsT_dve"), sem("rowsT_act")]
        s_gdr, s_sig, s_gs = sem("gate_read"), sem("sigmoid_ready"), sem("gate_ready")
        s_udr, s_pr = sem("up_read"), sem("activations_ready")
        s_yev, s_ty, s_yb = sem("yT_in_sbuf"), sem("y_transposed"), sem("y_weighted")
        s_sc, s_scd = [sem(f"scattered_tile{n}") for n in range(2)], sem("scattered")
        s_al = [sem(f"moe_output{q}_loaded") for q in range(QT)]
        s_fv, s_fr, s_fh, s_fo, s_out = sem("final_var"), sem("final_root"), sem("final_xhat"), sem("final_ready"), sem("stored")

        s_xgz = sem("gather_buffer_zeroed")
        s_past = sem("pool_past_waits")

        proj = [(True, KCC, kcT), (True, VCC, vcT)] + [(False, q, nat[:, q, :]) for q in range(QT)]
        proj += [(True, KSC, ksT), (True, KWC, kwT)]
        proj += [(True, QI + P * j, qiT[:, j, :]) for j in range(4)]
        proj += [(True, QN + P * j, qnT[:, j, :]) for j in range(4)]
        proj += [(True, QD + P * j, qdT[:, j, :]) for j in range(4)]
        NPJ = len(proj)

        def w_in_part(col):
            return {QI: 1, QD: 3}.get(col, 2 if col < KCC else 0)

        def last_unit(m):
            return 8 * m + 7 if m < NH else 64 + 4 * (m - NH) + 3

        def pj_scale(i):
            return -0.125 if (i >= 12) else None

        def pj_wait(eng, i):
            eng.wait_ge(s_pev[i % 2], i // 2 + 1)

        blocks = ExitStack()
        block = blocks.enter_context(nc.Block())

        @block.sync
        def _(sp):
            def load(name, dst, src):
                sp.dma_start(dst, src).then_inc(loaded(name), 16)
            def row_load(n, src):
                load(f"rows{n // 4}", rows[n], src.to_broadcast([P, D]))

            def ada_load(n):
                c0 = (2, 2, 4, 4, 3, 3, 5, 5)[n] * D + (n % 2) * 512
                load(f"ada{n // 2}", ada_half[n], a["w_ada"][0, :, c0:c0 + 512].rearrange("(k p) n -> p k n", p=P))
            load("cst", cst[:, :], a["k_cst"])
            load("onehot", onehot, a["k_onehot"])
            load("tab", tab[0:N_BUCKETS, :], a["rel_bias"])
            with nc.allow_non_contiguous_dma(reason="small vectors with features on partitions"):
                load("c", cT, a["c"].rearrange("b (k p) -> p (b k)", p=P))
                load("bada", badaT, a["b_ada"][:, 0:2 * D].rearrange("b (k p) -> p (b k)", p=P))
            load("x", xn, a["x"].rearrange("b (q p) n -> p (b q) n", p=P))
            for half in range(2):
                load(f"ada1_{half}", ada1[:, :, half * D:(half + 1) * D],
                     a["w_ada"][0, :, half * D:(half + 1) * D].rearrange("(k p) n -> p k n", p=P))
            with nc.allow_non_contiguous_dma(reason="small vectors with features on partitions"):
                for s, n in enumerate(("cmp_k_pos", "cmp_v_pos")):
                    load("small", pos2[:, s, :], a[n][0].rearrange("(l p2) d -> (p2 d) l", p2=2))
                load("small", ckvg, a["ckv_gain"].rearrange("a p -> p a"))
                for half in range(2):
                    hs = slice(half * DH, (half + 1) * DH)
                    load("small", kig[hs], a["kidx_gain"].rearrange("a p -> p a"))
                    load("small", kib[hs], a["kidx_bias"].rearrange("a p -> p a"))
                load("small", og[:, 0:4], a["nsa_out_gain"].rearrange("a (k p) -> p (a k)", p=P))
                load("small", og[:, 4:8], a["dsa_out_gain"].rearrange("a (k p) -> p (a k)", p=P))
            for s, n in enumerate(("w_uk", "w_uv")):
                load("small", wukv[:, s], a[n][0].rearrange("h c d -> c h d"))
            for s, n in enumerate(("cmp_k_w2", "cmp_v_w2")):
                load("small", w2[:, s], a[n][0].rearrange("(f p) d -> p f d", p=P))
            for src, dst, w in W_IN_MOVES:
                load(f"w_in{w_in_part(dst)}", w_in[:, :, dst:dst + w],
                     a["w_in"][0, :, src:src + w].rearrange("(k p) n -> p k n", p=P))
            sp.wait_ge(s_bias_sb, 1)
            load("e_d", e_d, E_sb[:, :])
            sp.wait_ge(loaded("e_d"), 16)
            pj_wait(sp, 0)
            pj_wait(sp, 1)
            for s, src in enumerate((kcT, vcT)):
                for g in range(NG):
                    for lp in range(2):
                        sp.dma_start(X[lp * DH:(lp + 1) * DH, s, g, 0:T - 1],
                                     src[g * DH:(g + 1) * DH, lp:T - 1 + lp]).then_inc(s_X, 16)
            sp.wait_ge(s_proj, NPJ)
            for s, n in enumerate(("cmp_k_w1", "cmp_v_w1")):
                load("w1", w1[:, s], a[n][0].rearrange("(l p) f -> p l f", p=P))
            for m in range(16):
                if m == 4:
                    sp.wait_ge(s_hid, 1)
                    ada_load(0)
                    ada_load(1)
                    load("w_out", w_out, a["w_out"][0].rearrange("(k p) n -> p k n", p=P))
                if m == 12:
                    sp.wait_ge(s_S, 64)
                    row_load(0, a["b_ada"][:, 2 * D:3 * D])
                    row_load(1, a["b_ada"][:, 4 * D:5 * D])
                    row_load(2, a["b_ada"][:, 3 * D:4 * D])
                    row_load(3, a["ln1_gain"])
                if m >= 2:
                    sp.wait_ge(s_ttr, last_unit(m - 2) + 1)
                    sp.wait_ge(s_cSub, min(m - 1, NH))
                w = MW if m < 8 else T
                skewed = bass.AP(tensor=e_d.tensor, offset=m * EW + MW - w, ap=[[1, P], [1, w]])
                load(f"master{m % 2}", master[:, m % 2, 0:w], skewed)

            sp.wait_ge(s_S, NU)
            row_load(4, a["ln1_bias"])
            row_load(5, a["b_ada"][:, 5 * D:6 * D])
            row_load(6, a["ln2_gain"])
            row_load(7, a["ln2_bias"])
            sp.wait_ge(s_PV, NU)
            ada_load(2)
            ada_load(3)
            sp.wait_ge(s_oev, NU)
            load("w_rt", w_rt, a["w_router"][0].rearrange("(k p) n -> p k n", p=P))
            load("w_rt", b_rt, a["b_router"].to_broadcast([P, NE]))
            sp.wait_ge(s_row, 2)
            ada_load(4)
            ada_load(5)
            sp.wait_ge(s_mT, KC)
            load("x_again", x1, a["x"].rearrange("b (q p) n -> p (b q) n", p=P))
            sp.wait_ge(s_row, 4)
            ada_load(6)
            ada_load(7)
            names = ("w_gate", "w_up", "w_down")

            def expert_load(j, i, e):
                m, c0 = j * SC // KC, j * SC % KC * P
                sp.wait_ge(s_mm, i * 24 + SC * (j + 1))
                sp.dma_start(ringf[:, j * SC * D:(j + 1) * SC * D].rearrange("p (k n) -> p k n", k=KC),
                             a[names[m]][0, e, :, c0:c0 + SC * P].rearrange("a (k p) n -> p (a k) n", p=P)).then_inc(s_w[j], 16)
            for j in (0, 1):
                expert_load(j, 0, slice(0, 1))
            sp.wait_ge(s_row, 8)
            for n, name in enumerate(("b_gate", "b_up", "b_down")):
                load("b_exp", b_f32[:, n, :], a[name][0])
            for q in range(QT):
                sp.wait_ge(s_h2, q + 1)
                sp.dma_start(h2_d[q * P:(q + 1) * P, :], h2[:, q % 2, :]).then_inc(s_h2st[q % 2], 16)

            for j in (2, 3):
                expert_load(j, 0, slice(0, 1))
            sp.wait_ge(s_x1, QT)
            sp.wait_ge(s_tables, 1)
            sp.wait_ge(s_zst, 16 * QT)
            for n in range(2):
                sp.wait_ge(s_h2st[n], 32)
            sp.wait_ge(s_gd, 1)
            for j in (4, 5):
                expert_load(j, 0, slice(0, 1))
            n_rounds = sp.value_load(rounds_i[0:1, 0:1], min_val=1, max_val=NR)
            with sp.Fori(0, n_rounds * NE - 1) as before:
                for j in range(NSLOT):
                    expert_load(j, before + 1, ds((before + 1) % NE, 1))
            for q in range(QT):
                sp.wait_ge(s_fo, q + 1)
                sp.dma_start(out[0, q * P:(q + 1) * P, :], ft[:, q, :]).then_inc(s_out, 16)
            sp.wait_ge(s_out, 16 * QT)

        @block.gpsimd
        def _(pool):
            pool.wait_ge(loaded("cst"), 16)
            nc.gpsimd.memset(cone, 1.0)
            nc.gpsimd.tensor_copy(identb[:, :], ident).then_inc(s_idb, 1)
            pool.wait_ge(s_X, 16 * 8)
            pool.wait_ge(loaded("small"), 16 * 13)
            for s in range(2):
                for g in range(NG):
                    base = X[:, s, g, :]
                    for lh in range(2):
                        v = base[:, 16 * lh:16 * lh + 496].rearrange("p (c l m) -> p l c m", l=8, m=2)[:, :, :, 0]
                        nc.gpsimd.tensor_tensor(
                            blk[:, s, 8 * lh:8 * lh + 8, g, :], v,
                            pos2[:, s, 8 * lh:8 * lh + 8].unsqueeze(2).to_broadcast([P, 8, NCMP]),
                            ALU.add).then_inc(s_blk, 1)

            own = [0]

            def link(ins):
                own[0] += 1
                ins.then_inc(chain_s["pool"], 1)
                pool.wait_ge(chain_s["pool"], own[0])
            pool.wait_ge(s_S, NU)
            nc.gpsimd.tensor_copy(trib[:, :], cst[:, C_TRI:C_TRI + P]).then_inc(s_trib, 1)
            pool.wait_ge(s_sel, 3)
            nc.gpsimd.memset(zero, 0.0).then_inc(s_zero, 1)
            pool.wait_ge(s_zero, 1)
            for n in range(QT):
                pool.dma_start(acc_d[n * P:(n + 1) * P, :], zero).then_inc(s_zst, 16)
            pool.wait_ge(loaded("rows0"), 64)
            pool.wait_ge(loaded("rows1"), 64)
            pool.wait_ge(s_rowev, 6)
            link(nc.gpsimd.tensor_tensor(yt[:, 0, :], ln1b, sc2r, ALU.mult))
            nc.gpsimd.tensor_tensor(sc2r, sc2r, ln1g, ALU.mult)
            link(nc.gpsimd.tensor_tensor(sh2r, sh2r, yt[:, 0, :], ALU.add))
            nc.gpsimd.tensor_scalar(ln1g, ln1g, ALPHA, None, ALU.mult)
            nc.gpsimd.tensor_scalar(ln1b, ln1b, ALPHA, None, ALU.mult).then_inc(s_ab, 1)
            for q in range(QT):
                pool.wait_ge(s_xh, q + 1)
                pool.wait_ge(s_ab, 1)
                link(nc.gpsimd.tensor_tensor(x1[:, q, :], yt[:, q % 2, :], ln1g, ALU.mult))
                nc.gpsimd.tensor_tensor(x1[:, q, :], x1[:, q, :], ln1b, ALU.add).then_inc(s_x1, 1)

            pool.wait_ge(s_bTev, 2)
            nc.gpsimd.tensor_scalar(biasT[:, 1, :, :], biasT[:, 1, :, :], 1.0, None, ALU.add).then_inc(s_bready, 1)
            pool.wait_ge(s_y, QT)
            nc.gpsimd.tensor_copy(iota[:, 0:P], cst[:, C_IOTA:C_IOTA + P])
            nc.gpsimd.tensor_scalar(iota[:, P:2 * P], cst[:, C_IOTA:C_IOTA + P], float(P), None, ALU.add).then_inc(s_bready, 1)
            nc.gpsimd.memset(xg, 0.0).then_inc(s_xgz, 1)

            def gather(u):
                pool.sem_inc(s_past, 1)
                pool.indirect_dma_start(xg[:, u, :], None, h2_d, bass.IndirectOffsetOnAxis(ap=idx_g[:, u:u + 1], axis=0),
                                        bounds_check=T - 1, oob_is_err=False).then_inc(s_g[u], 16)

            def scatter(u):
                pool.sem_inc(s_past, 1)
                pool.indirect_dma_start(acc_d, bass.IndirectOffsetOnAxis(ap=idx_s[:, u:u + 1], axis=0), yb[:, u, :], None,
                                        bounds_check=T - 1, oob_is_err=False, compute_op=ALU.add).then_inc(s_sc[u], 16)

            def table(ap, i, low, high):
                return pool.value_load(ap[0:1, i], min_val=low, max_val=high)
            pool.wait_ge(s_h2st[0], 32)
            pool.wait_ge(s_h2st[1], 32)
            pool.wait_ge(s_zst, 16 * QT)
            pool.wait_ge(s_xgz, 1)
            pool.wait_ge(s_idx, 1)
            gather(0)
            with pool.If(table(held_i, slice(0, 1), 0, SL) > P):
                gather(1)
                pool.wait_ge(s_g[1], 16)
            pool.wait_ge(s_g[0], 16)
            pool.sem_inc(s_gd, 1)
            pool.sem_inc(s_scd, 1)
            n_rounds = pool.value_load(rounds_i[0:1, 0:1], min_val=1, max_val=NR)
            with pool.Fori(0, n_rounds) as rd:
                with pool.Fori(0, NE) as e:
                    i = rd * NE + e
                    pool.wait_ge(s_idx, i + 2)
                    pool.wait_ge(s_tx, i * 4 + 4)
                    gather(0)
                    with pool.If(table(held_i, ds(i + 1, 1), 0, SL) > P):
                        gather(1)
                        pool.wait_ge(s_g[1], table(fulls_i, ds(i + 1, 1), 16, 16 * 2 * NE))
                    pool.wait_ge(s_g[0], i * 16 + 32)
                    pool.sem_inc(s_gd, 1)
                    pool.wait_ge(s_yb, i * 4 + 8)
                    scatter(0)
                    pool.wait_ge(s_sc[0], i * 16 + 16)
                    with pool.If(table(held_i, ds(i, 1), 0, SL) > P):
                        scatter(1)
                        pool.wait_ge(s_sc[1], table(fulls_i, ds(i, 1), 16, 16 * 2 * NE))
                    pool.sem_inc(s_scd, 1)
            pool.sem_inc(s_past, 1)
            for q in range(QT):
                pool.dma_start(acc[:, q, :], acc_d[q * P:(q + 1) * P, :]).then_inc(s_al[q], 16)
            for q in (0, 2):
                pool.wait_ge(s_fh, q + 1)
                link(nc.gpsimd.tensor_tensor(ft[:, q, :], ft[:, q, :], ln2g, ALU.mult))
                pool.wait_ge(s_fo, q)
                nc.gpsimd.tensor_tensor(ft[:, q, :], ft[:, q, :], ln2b, ALU.add).then_inc(s_fo, 1)

        @block.tensor
        def _(pe):
            pe.wait_ge(loaded("onehot"), 16)
            pe.wait_ge(loaded("tab"), 16)
            pe.wait_ge(s_tab, 1)
            for n in range(2):
                nc.tensor.matmul(bank[n][0:16, :], tab[0:33, :], onehot[:, n * 512:(n + 1) * 512],
                                 start=True, stop=True).then_inc(s_bias, 1)
            pe.wait_ge(loaded("x"), 16)
            pe.wait_ge(loaded("cst"), 16)

            def x_transposes(k):
                for q in range(QT):
                    last = nc.tensor.transpose(XB[k][:, q * P:(q + 1) * P],
                                               xn[:, q, k * P:(k + 1) * P], ident)
                last.then_inc(s_xT, 1)
            for k in range(5):
                x_transposes(k)
            pe.wait_ge(s_bias_sb, 1)
            for k in range(5, 7):
                x_transposes(k)
            pe.wait_ge(s_silu, 2)
            for c in range(4):
                pe.wait_ge(loaded(f"ada1_{c // 2}"), 16)
                if c:
                    pe.wait_ge(s_arowev, c)
                for k in range(KC):
                    last = nc.tensor.matmul(bank[7][0:1, :], siluc[:, k:k + 1], ada1[:, k, c * 512:(c + 1) * 512],
                                            start=(k == 0), stop=(k == KC - 1))
                last.then_inc(s_arow, 1)
            pe.wait_ge(s_arowev, 4)
            for j in range(16):
                last = nc.tensor.matmul(bank[7][:, j:j + 1], ada_row1[:, j * P:(j + 1) * P], ident[0:1, 0:1], start=True, stop=True)
            last.then_inc(s_ada, 1)
            pe.wait_ge(s_hT, 1)
            x_transposes(7)
            pe.wait_ge(s_hT, 4)
            pe.wait_ge(s_hTa, 4)
            for i, (tr, where, _dst) in enumerate(proj):
                if i in (0, 8, 12, 16):
                    step = {0: 0, 8: 1, 12: 2, 16: 3}[i]
                    pe.wait_ge(loaded(f"w_in{step}"), 16 * sum(w_in_part(m[1]) == step for m in W_IN_MOVES))
                if i >= 4:
                    pj_wait(pe, i - 4)
                b = bank[i % 4]
                for k in range(KC):
                    if not tr:
                        last = nc.tensor.matmul(b[:, 0:NATW], hT[:, k, where * P:(where + 1) * P],
                                                w_in[:, k, NAT:NAT + NATW], start=(k == 0), stop=(k == KC - 1))
                        continue
                    last = nc.tensor.matmul(b[:, :], w_in[:, k, where:where + P], hT[:, k, :], start=(k == 0), stop=(k == KC - 1))
                last.then_inc(s_proj, 1)
            pe.wait_ge(s_nat, 1)
            for q in range(QT):
                nc.tensor.transpose(bank[4][:, q * P:(q + 1) * P], nat[:, q, N_CKV:N_CKV + P], ident)
                last = nc.tensor.transpose(bank[5][:, q * P:(q + 1) * P], kin[:, q, :], ident)
            last.then_inc(s_ctr, 1)
            pe.wait_ge(s_cev, 1)
            for j in range(4):
                if j >= 2:
                    pe.wait_ge(s_kvev, 2 * j - 3 + 0)
                nc.tensor.matmul(bank[6][:, :] if j % 2 == 0 else bank[4][:, :],
                                 wukv[:, 0, 2 * j:2 * j + 2, :], ckvT, start=True, stop=True).then_inc(s_kv, 1)
                if j >= 1:
                    pe.wait_ge(s_kvev, 2 * j - 1 + 1)
                nc.tensor.matmul(bank[7][:, :], ckvT[:, j * P:(j + 1) * P],
                                 wukv[:, 1, :, :], start=True, stop=True).then_inc(s_kv, 1)
            pe.wait_ge(s_cev, 2)
            for n in range(24):
                q, h = n // 8 + 1, n % 8
                if n >= 4:
                    pe.wait_ge(s_relu, n - 3)
                else:
                    pj_wait(pe, NPJ - 4 + n)
                hs = slice((h % 2) * DH, (h % 2 + 1) * DH)
                nc.tensor.matmul(bank[n % 4][:, 0:(q + 1) * P], qiT[hs, h // 2, q * P:(q + 1) * P],
                                 kiT[hs, 0:(q + 1) * P], start=True, stop=True).then_inc(s_is, 1)
            pe.wait_ge(s_blk, 8)
            pe.wait_ge(loaded("w1"), 32)
            pe.wait_ge(s_cev, 2)
            for s in range(2):
                for f in range(2):
                    for l in range(LC):
                        last = nc.tensor.matmul(bank[5][:, (2 * s + f) * 62:(2 * s + f + 1) * 62],
                                                w1[:, s, l, f * P:(f + 1) * P],
                                                blk[:, s, l, :, :].rearrange("p g c -> p (g c)"),
                                                start=(l == 0), stop=(l == LC - 1))
            last.then_inc(s_hid, 1)
            pe.wait_ge(s_gel, 1)
            pe.wait_ge(s_kvev, 8)
            for g in range(NG):
                for f in range(2):
                    nc.tensor.matmul(bank[6][g * DH:(g + 1) * DH, 0:NCMP], w2[:, 0, f, :],
                                     gelu[:, 0, f, g * NCMP:(g + 1) * NCMP], start=(f == 0), stop=(f == 1))
                for f in range(2):
                    last = nc.tensor.matmul(bank[7][0:NCMP, g * DH:(g + 1) * DH], gelu[:, 1, f, g * NCMP:(g + 1) * NCMP],
                                            w2[:, 1, f, :], start=(f == 0), stop=(f == 1))
            last.then_inc(s_cmp, 1)
            pe.wait_ge(s_cmpev, 2)
            pe.wait_ge(s_relu, 24)

            for s in range(NU + 4):
                if s < 64 and s % 8 == 0:
                    h = s // 8
                    g, j = h // 4, h % 4
                    gs = slice(g * DH, (g + 1) * DH)
                    if h:
                        pe.wait_ge(s_cO, h)
                    for q in range(QT):
                        last = nc.tensor.matmul(bank[7][:, q * NCMP:(q + 1) * NCMP], qnT[gs, j, q * P:(q + 1) * P],
                                                kcmpT[gs, :], start=True, stop=True)
                    last.then_inc(s_cS, 1)
                if s < NU:
                    b, h, q = UNITS[s]
                    n = (q + 1) * P
                    if s >= 3:
                        pe.wait_ge(s_ttr, s - 2)
                    if b == DSA:
                        hs = slice((h % 2) * DH, (h % 2 + 1) * DH)
                        lhs, rhs = qdT[hs, h // 2, q * P:(q + 1) * P], kdT[hs, h // 2, 0:n]
                        if q:
                            pe.wait_ge(s_sel, q)
                            pe.wait_ge(s_idb, 1)
                            nc.tensor.matmul(bank[s % 3][:, 0:n], identb[:, :], selm[:, q - 1, 0:n], start=True, stop=False)
                    else:
                        gs = slice((h // 4) * DH, (h // 4 + 1) * DH)
                        lhs = qnT[gs, h % 4, q * P:(q + 1) * P]
                        rhs = (ksT if b == SLC else kwT)[gs, 0:n]
                    nc.tensor.matmul(bank[s % 3][:, 0:n], lhs, rhs, start=not (b == DSA and q), stop=True).then_inc(s_S, 1)
                if s < 64 and s % 8 == 4:
                    pe.wait_ge(s_cN, s // 8 + 1)
                    for q in range(QT):
                        last = nc.tensor.transpose(bank[7][0:NCMP, q * P:(q + 1) * P], Pc[:, q, :], ident)
                    last.then_inc(s_cT, 1)
                if s < 64 and s % 8 == 5:
                    pe.wait_ge(s_cTev, s // 8 + 1)
                    for q in range(QT):
                        last = nc.tensor.matmul(bank[7][:, q * DH:(q + 1) * DH], PcT[:, q * P:(q + 1) * P],
                                                vcmp[:, s // 32, :], start=True, stop=True)
                    last.then_inc(s_cPV, 1)
                if 0 <= s - 2 < NU:
                    u = s - 2
                    q = UNITS[u][2]
                    pe.wait_ge(s_exp, u + 1)
                    if u >= 2:
                        pe.wait_ge(s_Tev, u - 1)
                    for kb in range(q + 1):
                        last = nc.tensor.transpose(bank[3 + u % 2][:, kb * P:(kb + 1) * P], Sb[:, u % 4, kb * P:(kb + 1) * P], ident)
                    last.then_inc(s_T, 1)
                if 0 <= s - 3 < NU:
                    u = s - 3
                    b, h, q = UNITS[u]
                    pe.wait_ge(s_Tev, u + 1)
                    if u >= 2:
                        pe.wait_ge(s_oev, u - 1)
                    for kb in range(q + 1):
                        if b == DSA:
                            v = vd[:, kb, h * DH:(h + 1) * DH]
                        else:
                            c0 = (N_VS if b == SLC else N_VW) + (h // 4) * DH
                            v = nat[:, kb, c0:c0 + DH]
                        last = nc.tensor.matmul(bank[5 + u % 2][:, 0:DH], PTs[:, u % 4, kb * P:(kb + 1) * P], v,
                                                start=(kb == 0), stop=(kb == q))
                    last.then_inc(s_PV, 1)


            def ada_row(n):
                pe.wait_ge(loaded(f"ada{n // 2}"), 32)
                if n >= 2:
                    pe.wait_ge(s_rowev, n - 1)
                for k in range(KC):
                    last = nc.tensor.matmul(bank[7 if n % 2 == 0 else 0][:, :], siluc[:, k:k + 1].to_broadcast([P, P]), ada_half[n][:, k, :],
                                            start=(k == 0), stop=(k == KC - 1))
                last.then_inc(s_row, 1)
            ada_row(0)
            ada_row(1)
            pe.wait_ge(s_osc, 8)
            for k in range(KC):
                if k >= 4:
                    pe.wait_ge(s_mTev[k % 2], (k - 4) // 2 + 1)
                for q in range(QT):
                    last = nc.tensor.transpose(bank[1 + k % 4][:, q * P:(q + 1) * P], o[:, q, k * P:(k + 1) * P], ident)
                last.then_inc(s_mT, 1)
            for n in (2, 3, 4, 5):
                ada_row(n)
            pe.wait_ge(s_row, 6)
            pe.sem_inc(s_mm, 8)
            pe.wait_ge(loaded("w_out"), 16)
            pe.wait_ge(s_mTev[0], 4)
            pe.wait_ge(s_mTev[1], 4)
            def router(q):
                pe.wait_ge(s_h2, q + 1)
                if q:
                    pe.wait_ge(s_rTev, 2 * q)
                for k in range(KC):
                    last = nc.tensor.transpose(bank[5 + k // 4][:, (k % 4) * P:(k % 4 + 1) * P], h2[:, q % 2, k * P:(k + 1) * P], ident)
                last.then_inc(s_rT, 1)
                pe.wait_ge(s_rTev, 2 * q + 2)
                if q:
                    pe.wait_ge(s_rlv, q)
                for k in range(KC):
                    last = nc.tensor.matmul(bank[7][:, 0:NE], h2T[:, k, :], w_rt[:, k, :], start=(k == 0), stop=(k == KC - 1))
                last.then_inc(s_rl, 1)
            for q in range(QT):
                if q == 2:
                    ada_row(6)
                    ada_row(7)
                if q >= 2:
                    pe.wait_ge(s_yrd, q - 1)
                for k in range(KC):
                    for n in range(2):
                        last = nc.tensor.matmul(bank[1 + 2 * (q % 2) + n][:, :], mixT[:, k, q * P:(q + 1) * P], w_out[:, k, n * 512:(n + 1) * 512],
                                                start=(k == 0), stop=(k == KC - 1))
                last.then_inc(s_y, 1)
                if q == 2:
                    pe.wait_ge(loaded("w_rt"), 32)
                    pe.wait_ge(s_rowev, 8)
                    router(0)
            pe.wait_ge(s_y, QT)
            pe.sem_inc(s_mm, 8)
            router(1)
            pe.wait_ge(loaded("b_exp"), 48)
            pe.wait_ge(s_yrd, 3)
            for n in range(3 * KC):
                last = nc.tensor.transpose(bank[1 + n // 12][:, (n % 12) * NE:(n % 12 + 1) * NE],
                                           b_f32[:, n // KC, (n % KC) * P:(n % KC + 1) * P], ident[0:NE, 0:NE])
            last.then_inc(s_bT, 1)
            router(2)
            router(3)
            pe.wait_ge(s_selb, QT)
            pe.wait_ge(s_trib, 1)
            for q in range(QT):
                for q2 in range(q + 1):
                    nc.tensor.matmul(bank[5][:, q * NE:(q + 1) * NE], trib[:, :] if q2 == q else cone[:, 0:P], selb[:, q2, :],
                                     start=(q2 == 0), stop=(q2 == q))
            for q in range(QT):
                last = nc.tensor.matmul(bank[6][:, 0:NE], cone[:, 0:P], selb[:, q, :], start=(q == 0), stop=(q == QT - 1))
            last.then_inc(s_pos, 1)
            pe.wait_ge(s_tables, 1)
            pe.sem_inc(s_mm, 8)

            def slots(e):
                for u in range(2):
                    for q in range(QT):
                        last = nc.tensor.matmul(bank[5][:, 6 * u:6 * u + 6], OH[:, q, u * P:(u + 1) * P], TG[:, q, e, :],
                                                start=(q == 0), stop=(q == QT - 1))
                last.then_inc(s_rtm, 1)

            def rows_transposed(u):
                for half in range(2):
                    for c in range(4):
                        k = 4 * half + c
                        last = nc.tensor.transpose(bank[4 + 2 * u + half][:, c * P:(c + 1) * P], xg[:, u, k * P:(k + 1) * P], ident)
                    last.then_inc(s_tx, 1)

            def products(m, f, src, n):
                slot, c = (m * KC + f) // SC, (m * KC + f) % SC * P
                w = ringf[:, slot * SC * D:(slot + 1) * SC * D].rearrange("p (k n) -> p k n", k=KC)
                for k in range(KC):
                    last = nc.tensor.matmul(bank[f % 4][:, 0:n], w[:, k, c:c + P], src[:, k, 0:n],
                                            start=(k == 0), stop=(k == KC - 1))
                last.then_inc(s_mm, 1)

            def expert(i, e, n):
                def weights(m, f):
                    if f % SC == 0:
                        pe.wait_ge(s_w[(m * KC + f) // SC], i * 16 + 16)
                pe.wait_ge(s_xe[0], i * 2 + 2)
                pe.wait_ge(s_xe[1], i * 2 + 2)
                for f in range(KC):
                    weights(0, f)
                    if f < 4:
                        pe.wait_ge(s_yev, i * 8 + f + 5)
                    else:
                        pe.wait_ge(s_gdr, i * 8 + f - 3)
                    products(0, f, hTe, n)
                for f in range(KC):
                    weights(1, f)
                    if f < 4:
                        pe.wait_ge(s_gdr, i * 8 + f + 5)
                    else:
                        pe.wait_ge(s_udr, i * 8 + f - 3)
                    products(1, f, hTe, n)
                pe.wait_ge(s_gd, i + 2)
                rows_transposed(0)
                pe.wait_ge(s_yb, i * 4 + 4)
                rows_transposed(1)
                for f in range(KC):
                    weights(2, f)
                    if f < 4:
                        pe.wait_ge(s_udr, i * 8 + f + 5)
                    else:
                        pe.wait_ge(s_yev, i * 8 + f + 5)
                    if f == 0:
                        pe.wait_ge(s_pr, i * 8 + 8)
                    products(2, f, prod, n)
                for g in range(4):
                    u, half = g % 2, g // 2
                    if g == 2:
                        pe.wait_ge(s_xe[1], i * 2 + 3)
                        pe.wait_ge(s_oh, i + 3)
                        slots(ds(e + 2, 1))
                    if n <= P and u:
                        continue
                    if g < 2:
                        pe.wait_ge(s_xe[g], i * 2 + 4)
                    pe.wait_ge(s_yev, i * 8 + 12 + 4 * half)
                    pe.wait_ge(s_yb, i * 4 + g + 3)
                    for c in range(4):
                        last = nc.tensor.transpose(bank[6 + u][:, c * P:(c + 1) * P], yT[:, 4 * half + c, u * P:(u + 1) * P], ident)
                    last.then_inc(s_ty, 2 if n <= P else 1)

            pe.wait_ge(s_oh, 1)
            slots(slice(0, 1))
            pe.wait_ge(s_gd, 1)
            rows_transposed(0)
            rows_transposed(1)
            pe.wait_ge(s_xe[1], 2)
            pe.wait_ge(s_oh, 2)
            slots(slice(1, 2))
            n_rounds = pe.value_load(rounds_i[0:1, 0:1], min_val=1, max_val=NR)
            with pe.Fori(0, n_rounds) as rd:
                with pe.Fori(0, NE) as e:
                    i = rd * NE + e
                    tokens = pe.value_load(held_i[0:1, ds(i, 1)], min_val=0, max_val=SL)

                    def by_width(widths):
                        if len(widths) == 1:
                            expert(i, e, widths[0])
                            return
                        h = 1 if widths[0] == P else len(widths) // 2
                        with pe.If(tokens > widths[h - 1]):
                            by_width(widths[h:])
                        with pe.Else():
                            by_width(widths[:h])
                    by_width(WIDTHS)

        @block.scalar
        def _(act):
            act.wait_ge(loaded("c"), 16)
            nc.scalar.activation(siluc, cT, ACT.Sigmoid).then_inc(s_silu, 1)
            for c in range(4):
                act.wait_ge(s_arow, c + 1)
                nc.scalar.activation(ada_row1[:, c * 512:(c + 1) * 512], bank[7][0:1, :], ACT.Copy).then_inc(s_arowev, 1)
            act.wait_ge(s_adaT, 2)
            for k in (1, 3, 5, 7):
                act.wait_ge(s_xT, k + 1)
                nc.scalar.activation(hT[:, k, :], XB[k][:, :], ACT.Identity, bias=adaT[:, k:k + 1],
                                     scale=adaT[:, 8 + k:9 + k]).then_inc(s_hTa, 1)
            for i in range(1, NPJ, 2):
                act.wait_ge(s_proj, i + 1)
                dst = proj[i][2]
                src = bank[i % 4][:, 0:dst.shape[-1]]
                sc = pj_scale(i)
                nc.scalar.activation(dst, src, ACT.Copy, scale=1.0 if sc is None else sc).then_inc(s_pev[1], 1)
                if i == 5:
                    pj_wait(act, 4)
                    pj_wait(act, 5)
                    nc.scalar.activation(gsig, nat[:, :, N_GATE:N_GATE + 24], ACT.Sigmoid).then_inc(s_gsig, 1)
                    act.wait_ge(s_kvar, 1)
                    nc.scalar.activation(rs4, rs4, ACT.Sqrt).then_inc(s_sqrt, 1)
                    nc.scalar.activation(rk4, rk4, ACT.Sqrt).then_inc(s_sqrt, 1)
            act.wait_ge(s_ctr, 1)
            act.wait_ge(loaded("small"), 16 * 13)
            nc.scalar.activation(ckvT, bank[4][:, :], ACT.Copy, scale=ckvg).then_inc(s_cev, 1)
            nc.scalar.activation(kiT, bank[5][:, :], ACT.Identity, scale=kig, bias=kib).then_inc(s_cev, 1)
            for j in range(4):
                act.wait_ge(s_kv, 2 * j + 1)
                nc.scalar.activation(kdT[:, j, :], (bank[6] if j % 2 == 0 else bank[4])[:, :], ACT.Copy).then_inc(s_kvev, 1)
                act.wait_ge(s_kv, 2 * j + 2)
                nc.scalar.activation(vd[:, j, :], bank[7][:, :], ACT.Copy).then_inc(s_kvev, 1)
            for n in range(24):
                q = n // 8 + 1
                act.wait_ge(s_is, n + 1)
                if n >= 4:
                    act.wait_ge(s_isc, n - 3)
                else:
                    act.wait_ge(s_blk, 8)
                nc.scalar.activation(Sb[:, n % 4, :][:, 0:(q + 1) * P], bank[n % 4][:, 0:(q + 1) * P], ACT.Relu).then_inc(s_relu, 1)
            act.wait_ge(s_ga, 1)
            nc.scalar.activation(gt1[:, :, :, :], gt1[:, :, :, :], ACT.Tanh, scale=math.sqrt(2 / math.pi)).then_inc(s_gt, 1)
            for s in range(NU + 4):
                if s < NU:
                    n = (UNITS[s][2] + 1) * P
                    act.wait_ge(s_ttr, s + 1)
                    nc.scalar.activation(Sb[:, s % 4, 0:n], Sb[:, s % 4, 0:n], ACT.Exp, scale=-1.0, bias=umin[:, s:s + 1],
                                         accum_out=usum[:, s:s + 1]).then_inc(s_exp, 1)
                if s < 64 and s % 8 == 1:
                    act.wait_ge(s_cSub, s // 8 + 1)
                    nc.scalar.activation(Pc, Pc, ACT.Exp, scale=-1.0).then_inc(s_cExp, 1)
                if s < 64 and s % 8 == 4:
                    act.wait_ge(s_cT, s // 8 + 1)
                    nc.scalar.activation(PcT, bank[7][0:NCMP, :], ACT.Copy).then_inc(s_cTev, 1)
                if 0 <= s - 2 < NU:
                    u = s - 2
                    n = (UNITS[u][2] + 1) * P
                    act.wait_ge(s_T, u + 1)
                    if u >= 4:
                        act.wait_ge(s_PV, u - 3)
                    nc.scalar.activation(PTs[:, u % 4, 0:n], bank[3 + u % 2][:, 0:n], ACT.Copy).then_inc(s_Tev, 1)

            act.wait_ge(s_oev, NU)
            act.wait_ge(s_cO, NH)
            for n in range(8):
                nc.scalar.activation(yt[:, 0, 0:512] if n % 2 else yt[:, 0, 512:1024], o[:, n // 2, (n % 2) * 512:(n % 2 + 1) * 512], ACT.Square,
                                     accum_out=ssq[:, n:n + 1]).then_inc(s_ssq, 1)
                act.wait_ge(s_ssq, n + 1)
            act.wait_ge(s_ms, 1)
            nc.scalar.activation(rr8, rr8, ACT.Sqrt).then_inc(s_rt, 1)
            for k in range(1, KC, 2):
                act.wait_ge(s_mT, k + 1)
                nc.scalar.activation(mixT[:, k, :], bank[1 + k % 4][:, :], ACT.Copy, scale=og[:, k:k + 1]).then_inc(s_mTev[1], 1)
            def h2T_evac(q):
                act.wait_ge(s_rT, q + 1)
                if q:
                    act.wait_ge(s_rl, q)
                for n in range(2):
                    nc.scalar.activation(h2T[:, 4 * n:4 * n + 4, :], bank[5 + n][:, :].rearrange("p (k t) -> p k t", k=4), ACT.Copy).then_inc(s_rTev, 1)
            for q in range(QT):
                if q >= 2:
                    h2T_evac(q - 2)
                act.wait_ge(s_lv, q + 1)
                nc.scalar.activation(lnr[:, 0, q:q + 1], lnr[:, 0, q:q + 1], ACT.Sqrt).then_inc(s_lr, 1)
            for n in range(2):
                act.wait_ge(s_bT, 1)
                nc.scalar.activation(att[:, 11264 + 384 * n:11264 + 384 * (n + 1)], bank[1 + n][:, 0:384], ACT.Copy).then_inc(s_bTev, 1)
            h2T_evac(2)
            h2T_evac(3)
            for q in range(QT):
                act.wait_ge(s_rnm, q + 1)
                nc.scalar.activation(ex4[:, q, :], lg[:, q, :], ACT.Exp, bias=rsm[:, 0, q:q + 1]).then_inc(s_rex, 1)

            def rowsT(before):
                for u in range(2):
                    act.wait_ge(s_tx, before * 4 + 2 * u + 2)
                    nc.scalar.activation(hTe[:, 4:8, u * P:(u + 1) * P], bank[5 + 2 * u][:, :].rearrange("p (k t) -> p k t", k=4), ACT.Copy).then_inc(s_xe[1], 1)
            act.sem_inc(s_yev, 8)
            act.sem_inc(s_yb, 4)
            rowsT(0)
            act.wait_ge(s_tables, 1)
            n_rounds = act.value_load(rounds_i[0:1, 0:1], min_val=1, max_val=NR)
            with act.Fori(0, n_rounds) as rd:
                with act.Fori(0, NE) as e:
                    i = rd * NE + e
                    for f in range(KC):
                        act.wait_ge(s_gdr, i * 8 + f + 1)
                        if f >= 2:
                            act.wait_ge(s_gs, i * 8 + f - 1)
                        nc.scalar.activation(sgm[:, f % 2, :], gcl[:, f % 2, :], ACT.Sigmoid, scale=1.702).then_inc(s_sig, 1)
                    rowsT(i + 1)
                    for f in range(KC):
                        act.wait_ge(s_mm, i * 24 + 24 + 16 + f + 1)
                        nc.scalar.activation(yT[:, f, :], bank[f % 4][:, 0:SL], ACT.Identity, bias=bcur[:, 2, f:f + 1]).then_inc(s_yev, 1)
                    act.wait_ge(s_idx, i + 2)
                    for g in range(4):
                        u, half = g % 2, g // 2
                        act.wait_ge(s_ty, i * 4 + g + 1)
                        nc.scalar.activation(yb[:, u, half * 512:(half + 1) * 512], bank[6 + u][:, :], ACT.Copy,
                                             scale=wgt[:, u:u + 1]).then_inc(s_yb, 1)
            for q in range(QT):
                act.wait_ge(s_fv, q + 1)
                nc.scalar.activation(lnr[:, 0, q:q + 1], lnr[:, 0, q:q + 1], ACT.Sqrt).then_inc(s_fr, 1)

        @block.vector
        def _(dve):
            own = [0]

            def link(ins):
                own[0] += 1
                ins.then_inc(chain_s["dve"], 1)
                dve.wait_ge(chain_s["dve"], own[0])

            dve.wait_ge(loaded("tab"), 16)
            nc.vector.memset(tab[32:33, :], 1.0).then_inc(s_tab, 1)
            dve.wait_ge(s_silu, 1)
            nc.vector.tensor_tensor(siluc, siluc, cT, ALU.mult).then_inc(s_silu, 1)
            for n in range(2):
                dve.wait_ge(s_bias, n + 1)
                last = nc.vector.tensor_copy(E_sb[:, n * 512:(n + 1) * 512], bank[n][0:16, :])
            last.then_inc(s_bias_sb, 1)
            dve.wait_ge(s_ada, 1)
            dve.wait_ge(loaded("bada"), 16)
            nc.vector.tensor_tensor(adaT[:, 0:8], bank[7][:, 0:8], badaT[:, 0:8], ALU.add).then_inc(s_adaT, 1)
            nc.vector.scalar_tensor_tensor(adaT[:, 8:16], bank[7][:, 8:16], 1.0, badaT[:, 8:16], ALU.add, ALU.add).then_inc(s_adaT, 1)
            dve.wait_ge(s_adaT, 2)
            for k in (0, 2, 4, 6):
                dve.wait_ge(s_xT, k + 1)
                nc.vector.tensor_scalar(hT[:, k, :], XB[k][:, :], adaT[:, 8 + k:9 + k], adaT[:, k:k + 1],
                                        ALU.mult, ALU.add).then_inc(s_hT, 1)
            for i in range(0, NPJ, 2):
                dve.wait_ge(s_proj, i + 1)
                dst = proj[i][2]
                src = bank[i % 4][:, 0:dst.shape[-1]]
                sc = pj_scale(i)
                if sc is None:
                    nc.vector.tensor_copy(dst, src).then_inc(s_pev[0], 1)
                else:
                    nc.vector.tensor_scalar(dst, src, sc, None, ALU.mult).then_inc(s_pev[0], 1)
                if i == 4:
                    pj_wait(dve, 3)
                    pj_wait(dve, 4)
                    pj_wait(dve, 5)
                    for q in range(QT):
                        c = nat[:, q, N_CKV:N_CKV + P]
                        nc.vector.tensor_tensor_reduce(out=score[:, q * P:(q + 1) * P], in0=c, in1=c, scale=1.0, scalar=0.0,
                                                       op0=ALU.mult, op1=ALU.add, accum_out=ss4[:, q:q + 1])
                        last = nc.vector.bn_stats(st[:, q, :], nat[:, q, N_KI:N_KI + DH])
                    link(last)
                    for q in range(QT):
                        last = nc.vector.bn_aggr(mv[:, q, :], st[:, q, :])
                    nc.vector.tensor_scalar(rs4, ss4, 1.0 / P, 1e-6, ALU.mult, ALU.add)
                    link(last)
                    nc.vector.tensor_scalar(rk4, mv[:, :, 1], 1e-5, None, ALU.add).then_inc(s_kvar, 1)
                    nc.vector.tensor_scalar(wis, nat[:, :, N_WI:N_WI + NH], 8 ** -0.5 * DH ** -0.5, None, ALU.mult)
                    dve.wait_ge(s_sqrt, 2)
                    nc.vector.reciprocal(rs4, rs4)
                    link(nc.vector.reciprocal(rk4, rk4))
                    for q in range(QT):
                        c = nat[:, q, N_CKV:N_CKV + P]
                        nc.vector.tensor_scalar(c, c, rs4[:, q:q + 1], None, ALU.mult)
                        for half in range(2):
                            last = nc.vector.tensor_scalar(kin[:, q, half * DH:(half + 1) * DH], nat[:, q, N_KI:N_KI + DH],
                                                           mv[:, q, 0:1], rk4[:, q:q + 1], ALU.subtract, ALU.mult)
                    last.then_inc(s_nat, 1)
            dve.wait_ge(s_gsig, 1)
            dve.wait_ge(s_idb, 1)
            for n in range(24):
                q, h = n // 8 + 1, n % 8
                w = (q + 1) * P
                dve.wait_ge(s_relu, n + 1)
                sc = sel_s[:, q - 1, 0:w]
                if h == 0:
                    last = nc.vector.tensor_scalar(sc, Sb[:, n % 4, :][:, 0:w], wis[:, q, h:h + 1], None, ALU.mult)
                else:
                    dve.wait_ge(s_isc, n)
                    last = nc.vector.scalar_tensor_tensor(sc, Sb[:, n % 4, :][:, 0:w], wis[:, q, h:h + 1], sc, ALU.mult, ALU.add)
                last.then_inc(s_isc, 1)
                if h == 7:
                    dve.wait_ge(s_isc, n + 1)
                    link(nc.vector.tensor_tensor(sel_s[:, q - 1, q * P:(q + 1) * P], sel_s[:, q - 1, q * P:(q + 1) * P],
                                                 cst[:, C_CAUS:C_CAUS + P], ALU.add))
            dve.wait_ge(s_hid, 1)
            hid = bank[5][:, 0:248]
            g2 = gelu[:, :, :, :].rearrange("p a b c -> p (a b c)")
            g1 = gt1[:, :, :, :].rearrange("p a b c -> p (a b c)")
            link(nc.vector.tensor_copy(g2, hid))
            link(nc.vector.tensor_tensor(g1, g2, g2, ALU.mult))
            link(nc.vector.tensor_scalar(g1, g1, 0.044715, 1.0, ALU.mult, ALU.add))
            nc.vector.tensor_tensor(g1, g1, g2, ALU.mult).then_inc(s_ga, 1)
            dve.wait_ge(s_gt, 1)
            link(nc.vector.tensor_scalar(g1, g1, 0.5, 0.5, ALU.mult, ALU.add))
            nc.vector.tensor_tensor(g2, g2, g1, ALU.mult).then_inc(s_gel, 1)
            dve.wait_ge(s_cmp, 1)
            nc.vector.tensor_copy(kcmpT[:, :], bank[6][:, 0:NCMP]).then_inc(s_cmpev, 1)
            nc.vector.tensor_copy(vcmp[:, :, :], bank[7][0:NCMP, 0:128].rearrange("p (g d) -> p g d", g=2)).then_inc(s_cmpev, 1)

            def topk_round(n):
                q, r = n // 16 + 1, n % 16
                w = (q + 1) * P
                sc = sel_s[:, q - 1, 0:w]
                link(nc.vector.max(max8, sc if r == 0 else work[:, 0:w]))
                if r < 15:
                    link(nc.vector.match_replace(work[:, 0:w], max8, sc if r == 0 else work[:, 0:w], -3e38))
                    return
                gt, eq = score[:, 0:w], work[:, 0:w]
                nc.vector.tensor_scalar(eq, sc, max8[:, 7:8], None, ALU.is_equal)
                link(nc.vector.tensor_scalar(gt, sc, max8[:, 7:8], 0.0, ALU.is_gt, ALU.add, accum_out=cnt))
                nc.vector.tensor_scalar(need, cnt, -1.0, float(TOPK_KEYS), ALU.mult, ALU.add)
                link(nc.vector.tensor_tensor_scan(sc, cone[:, 0:w], eq, 0.0, ALU.mult, ALU.add))
                link(nc.vector.scalar_tensor_tensor(sc, sc, need, eq, ALU.is_le, ALU.mult))
                link(nc.vector.tensor_tensor(sc, sc, gt, ALU.add))
                nc.vector.tensor_scalar(selm[:, q - 1, 0:w], sc, -BIG, BIG, ALU.mult, ALU.add).then_inc(s_sel, 1)

            for s in range(NU + 5):
                if s < NU:
                    b, h, q = UNITS[s]
                    n = (q + 1) * P
                    m = h + (8 if b == DSA else 0)
                    dve.wait_ge(loaded(f"master{m % 2}"), 16 * (m // 2 + 1))
                    dve.wait_ge(s_S, s + 1)
                    if s >= 4:
                        dve.wait_ge(s_T, s - 3)
                    y0 = T - 1 + q * P - (MW - T if b == DSA else 0)
                    biases = bass.AP(tensor=master[:, :, :].tensor, offset=(m % 2) * MW + y0,
                                     ap=[list(master[:, :, :].ap[0]), [-1, n]])
                    nc.vector.tensor_tensor_reduce(out=Sb[:, s % 4, 0:n], in0=bank[s % 3][:, 0:n],
                                                   in1=biases, scale=1.0, scalar=3e38,
                                                   op0=ALU.add, op1=ALU.min, accum_out=umin[:, s:s + 1]).then_inc(s_ttr, 1)
                if s < 64 and s % 8 == 0:
                    h = s // 8
                    dve.wait_ge(s_cS, h + 1)
                    if h:
                        dve.wait_ge(s_cT, h)
                    y0 = T - CMP_LEN
                    mc = bass.AP(tensor=master[:, :, :].tensor, offset=(h % 2) * MW + y0,
                                 ap=[list(master[:, :, :].ap[0]), [P, QT], [-CMP_STRIDE, NCMP]])
                    link(nc.vector.tensor_tensor(Pc, bank[7][:, 0:QT * NCMP].rearrange("p (q c) -> p q c", q=QT), mc, ALU.add))
                    link(nc.vector.tensor_reduce(cm4[:, 0, :], Pc, AX.X, ALU.min))
                    nc.vector.tensor_tensor(Pc, Pc, cm4[:, 0, :].unsqueeze(2).to_broadcast([P, QT, NCMP]),
                                            ALU.subtract).then_inc(s_cSub, 1)
                if s < 64 and s % 8 == 2:
                    h = s // 8
                    dve.wait_ge(s_cExp, h + 1)
                    link(nc.vector.tensor_tensor(Pc, Pc,
                                                 cst[:, C_CMASK:C_CMASK + QT * NCMP].rearrange("p (q c) -> p q c", q=QT), ALU.mult))
                    link(nc.vector.tensor_reduce(cm4[:, 1, :], Pc, AX.X, ALU.add))
                    link(nc.vector.scalar_tensor_tensor(cm4[:, 2, :], cm4[:, 1, :], 0.0, cm4[:, 1, :], ALU.is_equal, ALU.add))
                    link(nc.vector.reciprocal(cm4[:, 3, :], cm4[:, 2, :]))
                    link(nc.vector.tensor_tensor(cm4[:, 3, :], cm4[:, 3, :], gsig[:, :, 3 * h], ALU.mult))
                    nc.vector.tensor_tensor(Pc, Pc, cm4[:, 3, :].unsqueeze(2).to_broadcast([P, QT, NCMP]),
                                            ALU.mult).then_inc(s_cN, 1)
                if 0 <= s - 8 < 48:
                    topk_round(s - 8)
                if 0 <= s - 4 < NU:
                    u = s - 4
                    b, h, q = UNITS[u]
                    dve.wait_ge(s_PV, u + 1)
                    r = rsum[:, u:u + 1]
                    link(nc.vector.reciprocal(r, usum[:, u:u + 1]))
                    ps = bank[5 + u % 2][:, 0:DH]
                    if b == DSA:
                        dst = o[:, q, 512 + h * DH:512 + (h + 1) * DH]
                    else:
                        dst = o[:, q, h * DH:(h + 1) * DH]
                        link(nc.vector.tensor_tensor(r, r, gsig[:, q, 3 * h + 1 + b:3 * h + 2 + b], ALU.mult))
                    if b != WIN:
                        nc.vector.tensor_scalar(dst, ps, r, None, ALU.mult).then_inc(s_oev, 1)
                    else:
                        dve.wait_ge(s_oev, u - 3)
                        dve.wait_ge(s_cO, h + 1)
                        nc.vector.scalar_tensor_tensor(dst, ps, r, dst, ALU.mult, ALU.add).then_inc(s_oev, 1)
                if s < 64 and s % 8 == 7:
                    h = s // 8
                    dve.wait_ge(s_cPV, h + 1)
                    dve.wait_ge(s_oev, 8 * h + 4)
                    oo = o[:, :, h * DH:(h + 1) * DH]
                    nc.vector.tensor_tensor(oo, oo, bank[7][:, 0:QT * DH].rearrange("p (q d) -> p q d", q=QT), ALU.add).then_inc(s_cO, 1)


            def ada_row(n):
                r = (0, 0, 1, 1, 2, 2, 5, 5)[n]
                dst = rows[r][:, (n % 2) * 512:(n % 2 + 1) * 512]
                dve.wait_ge(loaded(f"rows{r // 4}"), 64)
                dve.wait_ge(s_row, n + 1)
                nc.vector.scalar_tensor_tensor(dst, bank[7 if n % 2 == 0 else 0][:, :], 0.0 if r == 2 else 1.0, dst,
                                               ALU.add, ALU.add).then_inc(s_rowev, 1)
            dve.wait_ge(s_ssq, 8)
            nc.vector.tensor_scalar(rr8, ssq, 1.0 / 512, 1e-6, ALU.mult, ALU.add).then_inc(s_ms, 1)
            dve.wait_ge(s_rt, 1)
            link(nc.vector.reciprocal(rr8, rr8))
            for n in range(8):
                oo = o[:, n // 2, (n % 2) * 512:(n % 2 + 1) * 512]
                nc.vector.tensor_scalar(oo, oo, rr8[:, n:n + 1], None, ALU.mult).then_inc(s_osc, 1)
            ada_row(0)
            ada_row(1)
            for k in range(0, KC, 2):
                dve.wait_ge(s_mT, k + 1)
                nc.vector.tensor_scalar(mixT[:, k, :], bank[1 + k % 4][:, :], og[:, k:k + 1], None, ALU.mult).then_inc(s_mTev[0], 1)
            for n in (2, 3, 4, 5):
                ada_row(n)

            def statistics(src, q):
                for half in range(2):
                    last = nc.vector.bn_stats(lnst[:, q, half * 6:(half + 1) * 6], src[:, half * 512:(half + 1) * 512])
                link(last)
                link(nc.vector.bn_aggr(lnmv[:, q, :], lnst[:, q, :].rearrange("p (a b) -> p a b", a=2)))
                return nc.vector.tensor_scalar(lnr[:, 0, q:q + 1], lnmv[:, q, 1:2], 1e-5, None, ALU.add)
            def choice(q):
                dve.wait_ge(s_rl, q + 1)
                nc.vector.tensor_tensor(lg[:, q, :], bank[7][:, 0:NE], b_rt, ALU.add).then_inc(s_rlv, 1)
                dve.wait_ge(s_rlv, q + 1)
                link(nc.vector.max(m8[:, q, :], lg[:, q, :]))
                nc.vector.tensor_scalar(rsm[:, 0, q:q + 1], m8[:, q, 0:1], -1.0, None, ALU.mult).then_inc(s_rnm, 1)
                nc.vector.tensor_scalar(eq4[:, q, :], lg[:, q, :], m8[:, q, 3:4], None, ALU.is_equal)
                link(nc.vector.tensor_scalar(sel[:, q, :], lg[:, q, :], m8[:, q, 3:4], 0.0, ALU.is_gt, ALU.add, accum_out=rsm[:, 1, q:q + 1]))
                nc.vector.tensor_scalar(rsm[:, 2, q:q + 1], rsm[:, 1, q:q + 1], -1.0, float(TOPK_EXP), ALU.mult, ALU.add)
                link(nc.vector.tensor_tensor_scan(cum4[:, q, :], cone[:, 0:NE], eq4[:, q, :], 0.0, ALU.mult, ALU.add))
                link(nc.vector.scalar_tensor_tensor(cum4[:, q, :], cum4[:, q, :], rsm[:, 2, q:q + 1], eq4[:, q, :], ALU.is_le, ALU.mult))
                link(nc.vector.tensor_tensor(sel[:, q, :], sel[:, q, :], cum4[:, q, :], ALU.add))
                nc.vector.tensor_copy(selb[:, q, :], sel[:, q, :]).then_inc(s_selb, 1)
            dve.wait_ge(loaded("x_again"), 16)
            dve.wait_ge(s_rowev, 2)
            dve.wait_ge(s_ab, 1)
            for q in range(QT):
                dve.wait_ge(s_y, q + 1)
                t = yt[:, q % 2, :]
                if q >= 2:
                    dve.wait_ge(s_x1, q - 1)
                    dve.wait_ge(s_h2, q - 1)
                for half in range(2):
                    hs = slice(half * 512, (half + 1) * 512)
                    last = nc.vector.tensor_tensor(t[:, hs], bank[1 + 2 * (q % 2) + half][:, :], g1r[:, hs], ALU.mult)
                last.then_inc(s_yrd, 1)
                dve.wait_ge(s_yrd, q + 1)
                link(nc.vector.scalar_tensor_tensor(t, x1[:, q, :], ALPHA, t, ALU.mult, ALU.add))
                statistics(t, q).then_inc(s_lv, 1)
                dve.wait_ge(s_lr, q + 1)
                link(nc.vector.reciprocal(lnr[:, 1, q:q + 1], lnr[:, 0, q:q + 1]))
                nc.vector.tensor_scalar(t, t, lnmv[:, q, 0:1], lnr[:, 1, q:q + 1], ALU.subtract, ALU.mult).then_inc(s_xh, 1)
                dve.wait_ge(s_xh, q + 1)
                if q >= 2:
                    dve.wait_ge(s_h2st[q % 2], 16)
                    dve.wait_ge(s_rT, q - 1)
                link(nc.vector.tensor_tensor(h2[:, q % 2, :], t, sc2r, ALU.mult))
                nc.vector.tensor_tensor(h2[:, q % 2, :], h2[:, q % 2, :], sh2r, ALU.add).then_inc(s_h2, 1)
                if q == 1:
                    ada_row(6)
                    ada_row(7)
                    dve.wait_ge(loaded("w_rt"), 32)
                if q >= 2:
                    choice(q - 2)
            choice(2)
            choice(3)
            dve.wait_ge(loaded("cst"), 16)
            for q in range(QT):
                dve.wait_ge(s_rex, q + 1)
                link(nc.vector.tensor_tensor(ex4[:, q, :], ex4[:, q, :], sel[:, q, :], ALU.mult))
            link(nc.vector.tensor_reduce(rsm[:, 3, :], ex4, AX.X, ALU.add))
            link(nc.vector.reciprocal(rsm[:, 4, :], rsm[:, 3, :]))
            nc.vector.memset(TG, 1.0)
            link(nc.vector.memset(posr, -1.0))
            for q in range(QT):
                nc.vector.tensor_scalar(TG[:, q, :, 0], TG[:, q, :, 2], cst[:, C_TV:C_TV + 1], None, ALU.mult)
                last = nc.vector.tensor_scalar(ex4[:, q, :], ex4[:, q, :], rsm[:, 4, q:q + 1], None, ALU.mult)
            link(last)
            for q in range(QT):
                nc.vector.memset(TG[:, q, :, 1], float(P * q))
            nc.vector.memset(TG[:, :, :, 2], -float(NOWHERE))
            for n in (3, 4, 5):
                link(nc.vector.tensor_copy(TG[:, :, 0:NE, n], ex4))
                if n < 5:
                    link(nc.vector.tensor_tensor(ex4, ex4, TG[:, :, 0:NE, n], ALU.subtract))
            link(nc.vector.tensor_copy(TG[:, :, NE:NE + 2, :], TG[:, :, 0:2, :]))
            nc.vector.memset(held, 0.0)
            dve.wait_ge(s_pos, 1)
            link(nc.vector.scalar_tensor_tensor(cum4, bank[5][:, 0:128].rearrange("p (q e) -> p q e", q=QT), 1e4, sel, ALU.add, ALU.mult))
            for rd in range(NR):
                last = nc.vector.tensor_scalar(posr[:, :, rd * NE:(rd + 1) * NE], cum4, -1e4 - SL * rd, None, ALU.add)
            link(last)
            link(nc.vector.tensor_reduce(most[:, 0:1], bank[6][:, 0:NE], AX.X, ALU.max))
            link(nc.vector.tensor_scalar(most[:, 1:2], most[:, 0:1], float(SL), 1.0, ALU.is_gt, ALU.add))
            nc.vector.tensor_copy(rounds_i, most[:, 1:2])
            nc.vector.tensor_scalar(held[:, 0:NE], bank[6][:, 0:NE], float(SL), None, ALU.min)
            link(nc.vector.tensor_scalar(held[:, NE:2 * NE], bank[6][:, 0:NE], -float(SL), 0.0, ALU.add, ALU.max))
            nc.vector.tensor_copy(held_i, held)
            link(nc.vector.tensor_scalar(full, held, float(P), 16.0, ALU.is_gt, ALU.mult))
            link(nc.vector.tensor_tensor_scan(fulls, cone[:, 0:2 * NE + 1], full, 0.0, ALU.mult, ALU.add))
            nc.vector.tensor_copy(fulls_i, fulls).then_inc(s_tables, 1)
            dve.wait_ge(s_tables, 1)

            own_e = sem_e

            def one_hot(col):
                for q in range(QT):
                    last = nc.vector.tensor_scalar(OH[:, q, :], iota, posr[:, q, col], None, ALU.is_equal)
                last.then_inc(s_oh, 1)

            def slot_indices(before):
                parts = bank[5][:, 0:12].rearrange("p (u n) -> p u n", u=2)
                nc.vector.tensor_reduce(wnext, parts[:, :, 3:6], AX.X, ALU.add)
                nc.vector.tensor_reduce(slot_t, parts[:, :, 0:3], AX.X, ALU.add).then_inc(own_e, 1)
                dve.wait_ge(own_e, before + 1)
                nc.vector.tensor_scalar(idx_g, slot_t, float(NOWHERE), None, ALU.add).then_inc(s_idx, 1)

            def rowsT(before):
                for u in range(2):
                    dve.wait_ge(s_tx, before * 4 + 2 * u + 1)
                    nc.vector.tensor_copy(hTe[:, 0:4, u * P:(u + 1) * P], bank[4 + 2 * u][:, :].rearrange("p (k t) -> p k t", k=4)).then_inc(s_xe[0], 1)
            dve.wait_ge(s_bready, 2)
            one_hot(slice(0, 1))
            dve.wait_ge(s_rtm, 1)
            slot_indices(0)
            one_hot(slice(1, 2))
            rowsT(0)
            n_rounds = dve.value_load(rounds_i[0:1, 0:1], min_val=1, max_val=NR)
            OWN = 3
            with dve.Fori(0, n_rounds) as rd:
                with dve.Fori(0, NE) as e:
                    i = rd * NE + e
                    dve.wait_ge(s_yev, i * 8 + 8)
                    nc.vector.tensor_copy(bcur, biasT[:, :, :, ds(e, 1)].rearrange("p m k a -> p m (k a)")).then_inc(own_e, 1)
                    dve.wait_ge(own_e, i * OWN + 2)

                    def gated(f):
                        dve.wait_ge(s_sig, i * 8 + f + 1)
                        nc.vector.tensor_tensor(prod[:, f, :], gcl[:, f % 2, :], sgm[:, f % 2, :], ALU.mult).then_inc(s_gs, 1)
                    for f in range(KC):
                        dve.wait_ge(s_mm, i * 24 + 24 + f + 1)
                        if f >= 2:
                            dve.wait_ge(s_gs, i * 8 + f - 1)
                        nc.vector.tensor_scalar(gcl[:, f % 2, :], bank[f % 4][:, 0:SL], bcur[:, 0, f:f + 1], 7.0, ALU.add, ALU.min).then_inc(s_gdr, 1)
                        if f:
                            gated(f - 1)
                    gated(KC - 1)
                    dve.wait_ge(s_rtm, i + 2)
                    dve.wait_ge(s_gd, i + 1)
                    dve.wait_ge(s_scd, i + 1)
                    nc.vector.tensor_copy(idx_s, idx_g)
                    nc.vector.tensor_copy(wgt, wnext).then_inc(own_e, 1)
                    dve.wait_ge(own_e, i * OWN + 3)
                    slot_indices(i * OWN + 3)
                    dve.wait_ge(s_gs, i * 8 + 8)

                    def activation(f):
                        dve.wait_ge(s_udr, i * 8 + f + 1)
                        nc.vector.scalar_tensor_tensor(prod[:, f, :], ucl[:, f % 2, :], -6.0, prod[:, f, :], ALU.max, ALU.mult).then_inc(s_pr, 1)
                    for f in range(KC):
                        dve.wait_ge(s_mm, i * 24 + 24 + 8 + f + 1)
                        if f >= 2:
                            dve.wait_ge(s_pr, i * 8 + f - 1)
                        nc.vector.tensor_scalar(ucl[:, f % 2, :], bank[f % 4][:, 0:SL], bcur[:, 1, f:f + 1], 8.0, ALU.add, ALU.min).then_inc(s_udr, 1)
                        if f:
                            activation(f - 1)
                    activation(KC - 1)
                    one_hot(ds(i + 2, 1))
                    rowsT(i + 1)

            dve.wait_ge(loaded("rows1"), 64)
            for q in range(QT):
                dve.wait_ge(s_al[q], 16)
                t = ft[:, q, :]
                link(nc.vector.tensor_tensor(t, acc[:, q, :], g2r, ALU.mult))
                link(nc.vector.tensor_tensor(t, t, x1[:, q, :], ALU.add))
                statistics(t, q).then_inc(s_fv, 1)
                dve.wait_ge(s_fr, q + 1)
                link(nc.vector.reciprocal(lnr[:, 1, q:q + 1], lnr[:, 0, q:q + 1]))
                nc.vector.tensor_scalar(t, t, lnmv[:, q, 0:1], lnr[:, 1, q:q + 1], ALU.subtract, ALU.mult).then_inc(s_fh, 1)
                if q % 2:
                    dve.wait_ge(s_fh, q + 1)
                    link(nc.vector.tensor_tensor(t, t, ln2g, ALU.mult))
                    dve.wait_ge(s_fo, q)
                    nc.vector.tensor_tensor(t, t, ln2b, ALU.add).then_inc(s_fo, 1)
        blocks.close()


def constants():
    col = np.arange(EW)
    dist = col - (T - 1)
    d = np.maximum(dist, 1).astype(np.float32)
    large = 16 + (np.log(d / 16) / math.log(128 / 16) * 16).astype(np.int32)
    bucket = np.where(dist < 16, np.maximum(dist, 0), np.minimum(large, N_BUCKETS - 1))
    onehot = np.zeros((N_BUCKETS + 1, EW), np.float32)
    onehot[bucket[dist >= 0], col[dist >= 0]] = -1
    onehot[N_BUCKETS, dist < 0] = BIG
    cst = np.zeros((P, C_W), np.float32)
    p, n = np.arange(P)[:, None], np.arange(P)[None, :]
    cst[:, C_ID:C_ID + P] = p == n
    cst[:, C_TRI:C_TRI + P] = p < n
    cst[:, C_IOTA:C_IOTA + P] = n
    tok = np.arange(QT)[None, :, None] * P + p[:, :, None]
    key = np.arange(NCMP)[None, None, :] * CMP_STRIDE + CMP_LEN - 1
    cst[:, C_CMASK:C_CMASK + QT * NCMP] = (tok >= key).reshape(P, -1)
    cst[:, C_CAUS:C_CAUS + P] = np.where(n <= p, 0, -BIG)
    cst[:, C_TV:C_TV + QT] = np.arange(QT)[None, :] * P + p
    return {"k_cst": cst, "k_onehot": onehot}


def kernel(**inputs):
    import concourse.bacc as bacc
    from concourse.bass_utils import run_bass_kernel_spmd

    nc = bacc.Bacc("TRN2", target_bir_lowering=False, num_devices=1)
    arrays, aps = {}, {}
    for name, value in list(inputs.items()) + list(constants().items()):
        value = np.ascontiguousarray(value)
        arrays[f"in_{name}"] = value
        aps[name] = nc.dram_tensor(f"in_{name}", value.shape, mybir.dt.from_np(value.dtype), kind="ExternalInput").ap()
    out = nc.dram_tensor("out", (1, T, D), mybir.dt.float32, kind="ExternalOutput").ap()
    build_layer(nc, aps, out)
    r = run_bass_kernel_spmd(nc, [arrays], core_ids=[0])
    return r.results[0]["out"]
```
